# Optimizing a Trainium2 kernel written in Bass

```python
import math
import jax, jax.numpy as jnp
from jax import lax
import numpy as np

D_MODEL = 1024
BATCH = 1
SEQ = 1024
DEPTH = 1

HEAD_DIM = 64
N_Q_HEADS = 8
N_KV_HEADS = 2
Q_PER_KV = N_Q_HEADS // N_KV_HEADS
ATTN_WIDTH = N_Q_HEADS * HEAD_DIM
KV_WIDTH = N_KV_HEADS * HEAD_DIM
WINDOW = 128
ATTN_BLOCK = 128
N_BUCKETS = 32
MAX_DISTANCE = 128
GMLP_GROUPS = 8
GMLP_GROUP_DIM = 64
GMLP_WIDTH = GMLP_GROUPS * GMLP_GROUP_DIM
GMLP_CHUNK = 128
N_BRANCH = 2
IN_WIDTH = ATTN_WIDTH + 2 * KV_WIDTH + 2 * GMLP_WIDTH + N_BRANCH * D_MODEL
PEER_HEADS = 8
PEER_NKEYS = 128
PEER_N_EXPERTS = PEER_NKEYS * PEER_NKEYS
PEER_KEY_DIM = 256
PEER_HALF = PEER_KEY_DIM // 2
PEER_TOPK = 16
PEER_TOKEN_BLOCK = 128
EPS = 1e-6
NEG_INF = -1e30

kernel_name = "hybrid_swa_gmlp_peer_block"

def rmsnorm(x, w):
    xf = x.astype(jnp.float32)
    y = xf * lax.rsqrt(jnp.mean(xf * xf, axis=-1, keepdims=True) + EPS)
    return (y * w.astype(jnp.float32)).astype(x.dtype)

def layernorm(x, w, b):
    xf = x.astype(jnp.float32)
    mu = jnp.mean(xf, axis=-1, keepdims=True)
    xc = xf - mu
    y = xc * lax.rsqrt(jnp.mean(xc * xc, axis=-1, keepdims=True) + EPS)
    return (y * w.astype(jnp.float32) + b.astype(jnp.float32)).astype(x.dtype)

def t5_causal_bucket(dist):
    n = np.maximum(dist, 0)
    max_exact = N_BUCKETS // 2
    large = max_exact + (np.log(np.maximum(n, 1) / max_exact) / np.log(MAX_DISTANCE / max_exact)
                         * (N_BUCKETS - max_exact)).astype(np.int32)
    large = np.minimum(large, N_BUCKETS - 1)
    return np.where(n < max_exact, n, large).astype(np.int32)

def sliding_window_gqa(q, k, v, rel_bias, sinks):
    B, S = q.shape[0], q.shape[1]
    nb = S // ATTN_BLOCK
    q = q.reshape(B, nb, ATTN_BLOCK, N_KV_HEADS, Q_PER_KV, HEAD_DIM)
    k = k.reshape(B, nb, ATTN_BLOCK, N_KV_HEADS, HEAD_DIM)
    v = v.reshape(B, nb, ATTN_BLOCK, N_KV_HEADS, HEAD_DIM)

    def band(t):
        prev = jnp.pad(t, ((0, 0), (1, 0), (0, 0), (0, 0), (0, 0)))[:, :-1]
        return jnp.concatenate([prev, t], axis=2)

    kb, vb = band(k), band(v)
    logits = jnp.einsum('bnqhgd,bnshd->bnhgqs', q, kb).astype(jnp.float32) * (HEAD_DIM ** -0.5)

    qi = np.arange(ATTN_BLOCK)[:, None]
    kj = np.arange(2 * ATTN_BLOCK)[None, :]
    dist = qi + ATTN_BLOCK - kj
    bias = rel_bias.astype(jnp.float32)[t5_causal_bucket(dist)]
    bias = bias.transpose(2, 0, 1).reshape(N_KV_HEADS, Q_PER_KV, ATTN_BLOCK, 2 * ATTN_BLOCK)
    in_window = (dist >= 0) & (dist < WINDOW)
    key_exists = (np.arange(nb)[:, None, None] > 0) | (kj >= ATTN_BLOCK)[None]
    valid = in_window[None] & key_exists
    logits = jnp.where(valid[None, :, None, None], logits + bias, NEG_INF)

    sink = jnp.broadcast_to(sinks.astype(jnp.float32).reshape(N_KV_HEADS, Q_PER_KV)[None, None, :, :, None, None],
                            logits.shape[:-1] + (1,))
    probs = jax.nn.softmax(jnp.concatenate([logits, sink], axis=-1), axis=-1)[..., :-1]
    out = jnp.einsum('bnhgqs,bnshd->bnqhgd', probs.astype(vb.dtype), vb)
    return out.reshape(B, S, ATTN_WIDTH)

def chunked_spatial_gating(u, v, ln_w, ln_b, w_s, b_s):
    B, S = u.shape[0], u.shape[1]
    nc = S // GMLP_CHUNK
    v = layernorm(v, ln_w, ln_b).reshape(B, nc, GMLP_CHUNK, GMLP_GROUPS, GMLP_GROUP_DIM)
    causal = np.tril(np.ones((GMLP_CHUNK, GMLP_CHUNK), dtype=bool))
    w = jnp.where(causal[None], w_s, 0).astype(v.dtype)
    s = jnp.einsum('gts,bcsgd->bctgd', w, v) + b_s.T.astype(v.dtype)[None, None, :, :, None]
    y = u.reshape(B, nc, GMLP_CHUNK, GMLP_GROUPS, GMLP_GROUP_DIM) * s
    return y.reshape(B, S, GMLP_WIDTH)

def peer_ffn(x, w_q, keys_1, keys_2, u_tab, v_tab):
    B, S, D = x.shape
    q = (x @ w_q).reshape(B, S, PEER_HEADS, PEER_KEY_DIM)
    s1 = jnp.einsum('bshd,nd->bshn', q[..., :PEER_HALF], keys_1).astype(jnp.float32)
    s2 = jnp.einsum('bshd,nd->bshn', q[..., PEER_HALF:], keys_2).astype(jnp.float32)
    v1, i1 = lax.top_k(s1, PEER_TOPK)
    v2, i2 = lax.top_k(s2, PEER_TOPK)
    cand_s = (v1[..., :, None] + v2[..., None, :]).reshape(B, S, PEER_HEADS, PEER_TOPK * PEER_TOPK)
    cand_i = (i1[..., :, None] * PEER_NKEYS + i2[..., None, :]).reshape(B, S, PEER_HEADS, PEER_TOPK * PEER_TOPK)
    top_s, pos = lax.top_k(cand_s, PEER_TOPK)
    idx = jnp.take_along_axis(cand_i, pos, axis=-1)
    gate = jax.nn.softmax(top_s, axis=-1).astype(x.dtype)

    n_blk = (B * S) // PEER_TOKEN_BLOCK
    xs = x.reshape(n_blk, PEER_TOKEN_BLOCK, D)
    idxs = idx.reshape(n_blk, PEER_TOKEN_BLOCK, PEER_HEADS, PEER_TOPK)
    gates = gate.reshape(n_blk, PEER_TOKEN_BLOCK, PEER_HEADS, PEER_TOPK)

    def token_block(args):
        xb, ib, gb = args
        ue = u_tab[ib]
        act = jax.nn.gelu(jnp.einsum('thkd,td->thk', ue, xb)) * gb
        ve = v_tab[ib]
        return jnp.einsum('thk,thkd->td', act, ve)

    y = lax.map(token_block, (xs, idxs, gates))
    return y.reshape(B, S, D)

def setup_inputs(seed: int = 0) -> dict:
    key = jax.random.key(seed)
    ks = jax.random.split(key, 20)
    f32 = jnp.float32
    L, D = DEPTH, D_MODEL
    nrm = lambda k, shape, scale: jax.random.normal(k, shape, f32) * scale
    return {
        "x": nrm(ks[0], (BATCH, SEQ, D), 1.0),
        "mix_norm_w": 1.0 + nrm(ks[1], (L, D), 0.02),
        "w_in": nrm(ks[2], (L, D, IN_WIDTH), D ** -0.5),
        "rel_bias": nrm(ks[3], (N_BUCKETS, N_Q_HEADS), 0.3),
        "attn_sinks": nrm(ks[4], (L, N_Q_HEADS), 0.5),
        "w_branch_attn": nrm(ks[5], (L, ATTN_WIDTH, D), ATTN_WIDTH ** -0.5),
        "gmlp_ln_w": 1.0 + nrm(ks[6], (L, GMLP_WIDTH), 0.02),
        "gmlp_ln_b": nrm(ks[7], (L, GMLP_WIDTH), 0.02),
        "gmlp_w_s": nrm(ks[8], (L, GMLP_GROUPS, GMLP_CHUNK, GMLP_CHUNK), GMLP_CHUNK ** -0.5),
        "gmlp_b_s": 1.0 + nrm(ks[9], (L, GMLP_GROUPS, GMLP_CHUNK), 0.1),
        "w_branch_gmlp": nrm(ks[10], (L, GMLP_WIDTH, D), GMLP_WIDTH ** -0.5),
        "w_out": nrm(ks[11], (L, D, D), D ** -0.5),
        "ffn_norm_w": 1.0 + nrm(ks[12], (L, D), 0.02),
        "peer_w_q": nrm(ks[13], (L, D, PEER_HEADS * PEER_KEY_DIM), D ** -0.5),
        "peer_keys_1": nrm(ks[14], (L, PEER_NKEYS, PEER_HALF), PEER_HALF ** -0.5),
        "peer_keys_2": nrm(ks[15], (L, PEER_NKEYS, PEER_HALF), PEER_HALF ** -0.5),
        "peer_u": nrm(ks[16], (L, PEER_N_EXPERTS, D), D ** -0.5),
        "peer_v": nrm(ks[17], (L, PEER_N_EXPERTS, D), PEER_HEADS ** -0.5),
        "final_norm_w": 1.0 + nrm(ks[18], (D,), 0.02),
    }

def reference(x, mix_norm_w, w_in, rel_bias, attn_sinks, w_branch_attn, gmlp_ln_w, gmlp_ln_b,
              gmlp_w_s, gmlp_b_s, w_branch_gmlp, w_out, ffn_norm_w, peer_w_q, peer_keys_1,
              peer_keys_2, peer_u, peer_v, final_norm_w):
    B, S, D = x.shape
    splits = np.cumsum([ATTN_WIDTH, KV_WIDTH, KV_WIDTH, GMLP_WIDTH, GMLP_WIDTH, D_MODEL])
    for l in range(DEPTH):
        h = rmsnorm(x, mix_norm_w[l])
        z = h @ w_in[l]
        q, k, v, gu, gv, gate_a, gate_b = jnp.split(z, splits, axis=-1)
        y_a = sliding_window_gqa(q.reshape(B, S, N_Q_HEADS, HEAD_DIM),
                                 k.reshape(B, S, N_KV_HEADS, HEAD_DIM),
                                 v.reshape(B, S, N_KV_HEADS, HEAD_DIM),
                                 rel_bias, attn_sinks[l]) @ w_branch_attn[l]
        y_b = chunked_spatial_gating(jax.nn.gelu(gu), jax.nn.gelu(gv), gmlp_ln_w[l], gmlp_ln_b[l],
                                     gmlp_w_s[l], gmlp_b_s[l]) @ w_branch_gmlp[l]
        merged = jax.nn.sigmoid(gate_a) * y_a + jax.nn.sigmoid(gate_b) * y_b
        x = x + merged @ w_out[l]
        x = x + peer_ffn(rmsnorm(x, ffn_norm_w[l]), peer_w_q[l], peer_keys_1[l], peer_keys_2[l],
                         peer_u[l], peer_v[l])
    return rmsnorm(x, final_norm_w)


_drawn_inputs = setup_inputs


def setup_inputs(seed=0):
    import zlib

    import numpy as np

    out = dict(_drawn_inputs(seed))
    spreads = {}
    factors = {'attn_sinks': 8.0,
     'gmlp_ln_w': 13.036,
     'gmlp_ln_b': 12.83,
     'final_norm_w': 8.393,
     'rel_bias': 2.966,
     'ffn_norm_w': 3.121}
    for name, (base, spread) in spreads.items():
        noise = np.random.default_rng([zlib.crc32(name.encode()), seed]).standard_normal(out[name].shape)
        drawn = base * np.exp(spread * noise) if base else spread * noise
        out[name] = __import__('jax').numpy.asarray(drawn.astype(out[name].dtype))
    for name, factor in factors.items():
        out[name] = (out[name] * factor).astype(out[name].dtype)
    return out
```

```python
from contextlib import ExitStack

import numpy as np

import concourse.bass as bass
from concourse import mybir

ALU = mybir.AluOpType
ACT = mybir.ActivationFunctionType
AX = mybir.AxisListType
F32 = mybir.dt.float32
U32 = mybir.dt.uint32

P = 128
D = 1024
SEQ = 1024
TILES = SEQ // P
KO = D // P
HEADS = 8
KV_HEADS = 2
HD = 64
WIDTH = HEADS * HD
WB = WIDTH // P
BUCKETS = 32
MAX_DISTANCE = 128
EPS = 1e-6
NEG_INF = -1e30

GROUP = 512
GROUPS = SEQ // GROUP
GT = GROUP // P
BANKS = 4

SLOTS = 8
CHUNK = D
QKV_CHUNKS = WB + 2
ROUNDS = 6

N_HT = 0
N_Q = N_HT + KO
N_K = N_Q + WB
N_V = N_K + 1
N_GU = N_V + 1
N_GV = N_GU + WB
N_GATE = N_GV + GT
N_BRANCH = N_GATE + 2 * KO
N_OUT = N_BRANCH + 2 * KO
N_ALL = N_OUT + 2 * GT
GATES_PER_TILE = 2 * KO // GT

PH = 8
NKEYS = 128
TOPK = 16
RING = 8
BATCH = 2
BATCHES = TOPK // BATCH
LOWEST = -3.0e38

C_MIXW = 0
C_SINK = C_MIXW + KO
C_LNW = C_SINK + HEADS
C_LNB = C_LNW + WIDTH
C_BS = C_LNB + WIDTH
C_WS = C_BS + WB * P
C_IDENT = C_WS + HEADS * P
C_OWN01 = C_IDENT + P
C_PREV01 = C_OWN01 + P
C_OWNNEG = C_PREV01 + P
C_PREVNEG = C_OWNNEG + P
C_DIST = C_PREVNEG + P
C_REL = C_DIST + 2 * P
MIX_COLS = C_REL + HEADS
E_KEYS = 0
E_IDENT = E_KEYS + 2 * NKEYS
E_FFNW = E_IDENT + P
E_FINW = E_FFNW + D
E_IOTA = E_FINW + D
EXP_COLS = E_IOTA + TOPK


class Chain:

    def __init__(self, eng, sem):
        self.eng, self.sem, self.n = eng, sem, 0

    def mark(self, ins):
        self.n += 1
        return ins.then_inc(self.sem, 1)

    def wait(self):
        self.eng.wait_ge(self.sem, self.n)

    def step(self, ins):
        self.mark(ins)
        self.wait()

    def restart(self):
        self.eng.sem_clear(self.sem)
        self.n = 0


def mixer_block(nc, x_in, weights, mix_params, x2_out):
    with ExitStack() as ctx:
        def sb(name, shape, dt=F32):
            return ctx.enter_context(nc.sbuf_tensor(name, shape, dt))

        def sem(name):
            return ctx.enter_context(nc.semaphore(name))

        x = sb("x", [P, GT, D])
        hn = sb("hn", [P, GT, D])
        hT = sb("hT", [P, KO, GROUP])
        qT = sb("qT", [P, WB, GROUP])
        kT = sb("kT", [P, P + GROUP])
        vtok = sb("vtok", [P, GT + 1, P])
        guT = sb("guT", [P, WB, GROUP])
        gv = sb("gv", [P, GT, WIDTH])
        gates = sb("gates", [P, 2 * KO, GROUP])
        attnT = sb("attnT", [P, WB, GROUP])
        gmlpT = sb("gmlpT", [P, WB, GROUP])
        wring = sb("wring", [P, SLOTS, CHUNK])
        par = sb("par", [P, MIX_COLS])
        bias_own = sb("bias_own", [P, HEADS, P])
        bias_prev = sb("bias_prev", [P, HEADS, P])
        bias_first = sb("bias_first", [P, HEADS, P])
        probs = sb("probs", [P, HEADS * P + HEADS])
        pt_own = sb("pt_own", [P, HEADS, P])
        pt_prev = sb("pt_prev", [P, HEADS, P])
        ss = sb("ss", [P, GT])
        rms = sb("rms", [P, GT])
        rstd = sb("rstd", [P, GT])
        top = sb("top", [P, HEADS])
        den = sb("den", [P, HEADS])
        rden = sb("rden", [P, HEADS])
        stats = sb("stats", [P, GT, 6])
        mv = sb("mv", [P, GT, 2])
        ln_std = sb("ln_std", [P, GT])
        ln_rstd = sb("ln_rstd", [P, GT])
        eps = sb("eps", [P, 1])

        bank = ctx.enter_context(nc.psum_tensor("bank", [P, BANKS, GROUP], F32))
        logits = ctx.enter_context(nc.psum_tensor("logits", [P, HEADS, 2 * P], F32))
        lflat = logits[:].rearrange("p h j -> p (h j)")
        ptT = lflat[:, 0:HEADS * P].rearrange("p (h i) -> p h i", h=HEADS)
        pv = lflat[:, HEADS * P:HEADS * P + WB * P].rearrange("p (b i) -> p b i", b=WB)
        sg = lflat[:, HEADS * P + WB * P:HEADS * P + 2 * WB * P].rearrange("p (b i) -> p b i", b=WB)

        ident = par[:, C_IDENT:C_IDENT + P]

        params_in = sem("params_in")
        x_loaded = sem("x_loaded")
        w_loaded = [sem(f"w_loaded{s}") for s in range(SLOTS)]
        w_free = [sem(f"w_free{s}") for s in range(SLOTS)]
        consts_set = sem("consts_set")
        rms_ready = sem("rms_ready")
        hn_ready = sem("hn_ready")
        product_done = sem("product_done")
        act_taken = sem("act_taken")
        dve_taken = sem("dve_taken")
        rel_done = sem("rel_done")
        bias_ready = sem("bias_ready")
        carry_ready = sem("carry_ready")
        ln_var = sem("ln_var")
        ln_std_ready = sem("ln_std_ready")
        vln_ready = sem("vln_ready")
        logits_done = sem("logits_done")
        shifted_ready = sem("shifted_ready")
        exp_done = sem("exp_done")
        probs_ready = sem("probs_ready")
        pt_done = sem("pt_done")
        pt_masked = sem("pt_masked")
        pv_done = sem("pv_done")
        sg_done = sem("sg_done")
        branch_in = sem("branch_in")
        merged_ready = sem("merged_ready")
        x2_ready = sem("x2_ready")
        x2_stored = sem("x2_stored")
        x_free = sem("x_free")
        dve_chain = sem("dve_chain")
        act_chain = sem("act_chain")

        block = ctx.enter_context(nc.Block())

        def loads_before(s, g, r):
            return g * ROUNDS + r if s < QKV_CHUNKS else g * (ROUNDS - 1) + r - 1

        @block.sync
        def _(sp):
            sp.dma_start(par[:], mix_params).then_inc(params_in, 16)
            with sp.Fori(0, GROUPS) as g:
                sp.dma_start(x[:], x_in[bass.ds(g, 1)].rearrange("g p t d -> (g p) t d")).then_inc(x_loaded, 16)
                for s in range(QKV_CHUNKS):
                    sp.wait_ge(w_free[s], loads_before(s, g, 0) + 1)
                    sp.dma_start(wring[:, s, :], weights[s]).then_inc(w_loaded[s], 16)
                with sp.Fori(1, ROUNDS) as r:
                    for s in range(SLOTS):
                        chunk = sp.snap(r * SLOTS + s)
                        sp.wait_ge(w_free[s], loads_before(s, g, r) + 1)
                        sp.dma_start(wring[:, s, :], weights[bass.ds(chunk, 1)].rearrange(
                            "c p d -> (c p) d")).then_inc(w_loaded[s], 16)
                first_tile = sp.snap(g * GT)
                sp.wait_ge(x2_ready, g + 1)
                sp.dma_start(x2_out[bass.ds(first_tile, GT)].rearrange("t p d -> p t d"), x[:]).then_inc(x2_stored, 16)
                sp.wait_ge(x2_stored, 16 * g + 16)
                sp.sem_inc(x_free, 1)

        @block.tensor
        def _(pe):
            for s in range(SLOTS):
                pe.sem_inc(w_free[s], 1)
            pe.wait_ge(params_in, 16)
            rel = lflat[:, 0:HEADS * P].rearrange("p (j h) -> p j h", j=P)
            for j in range(P):
                last = pe.matmul(rel[:, j, :], par[0:BUCKETS, C_DIST + P - j:C_DIST + 2 * P - j],
                                 par[0:BUCKETS, C_REL:C_REL + HEADS], start=True, stop=True)
            last.then_inc(rel_done, 1)

            with pe.Fori(0, GROUPS) as g:
                def bank_free(n):
                    m = n - BANKS
                    if m >= N_BRANCH:
                        pe.wait_ge(dve_taken, g * (N_ALL - N_BRANCH) + (m - N_BRANCH + 1))
                    elif m >= 0:
                        pe.wait_ge(act_taken, g * N_BRANCH + (m + 1))

                def chunk_in(r, s):
                    pe.wait_ge(w_loaded[s], loads_before(s, g, r) * 16 + 16)

                used = []

                def release(ins):
                    if used:
                        ins.then_inc(w_free[used.pop()], 1)

                def rows_of_weights(n, r, s):
                    chunk_in(r, s)
                    bank_free(n)
                    w = wring[:, s, :].rearrange("p (k m) -> p k m", k=KO)
                    for k in range(KO):
                        last = pe.matmul(bank[:, n % BANKS, :], w[:, k, :], hT[:, k, :],
                                         start=(k == 0), stop=(k == KO - 1))
                        if k == 0:
                            release(last)
                    last.then_inc(product_done, 1)
                    used.append(s)

                for k in range(KO):
                    n = N_HT + k
                    bank_free(n)
                    for t in range(GT):
                        if k == 0:
                            pe.wait_ge(hn_ready, g * GT + t + 1)
                        last = pe.transpose(bank[:, n % BANKS, t * P:(t + 1) * P], hn[:, t, k * P:(k + 1) * P], ident)
                    last.then_inc(product_done, 1)

                pe.wait_ge(act_taken, g * N_BRANCH + (N_HT + KO))
                for b in range(WB + 1):
                    rows_of_weights(N_Q + b, 0, b)
                chunk_in(0, WB + 1)
                bank_free(N_V)
                wv = wring[:, WB + 1, :].rearrange("p (k m) -> p k m", k=KO)
                for t in range(GT):
                    for k in range(KO):
                        last = pe.matmul(bank[:, N_V % BANKS, t * P:(t + 1) * P], hT[:, k, t * P:(t + 1) * P], wv[:, k, :],
                                         start=(k == 0), stop=(k == KO - 1))
                        if t == 0 and k == 0:
                            release(last)
                last.then_inc(product_done, 1)
                used.append(WB + 1)
                for b in range(WB):
                    rows_of_weights(N_GU + b, 1, b)
                for c in range(4):
                    chunk_in(1, WB + c)
                    w = wring[:, WB + c, :].rearrange("p (k m) -> p k m", k=2)
                    for t in range(GT):
                        if c == 0:
                            bank_free(N_GV + t)
                        for k in range(2):
                            last = pe.matmul(bank[:, (N_GV + t) % BANKS, :], hT[:, 2 * c + k, t * P:(t + 1) * P], w[:, k, :],
                                             start=(c == 0 and k == 0), stop=(c == 3 and k == 1))
                            if t == 0 and k == 0:
                                release(last)
                        if c == 3:
                            last.then_inc(product_done, 1)
                    used.append(WB + c)

                for t in range(GT):
                    pe.wait_ge(act_taken, g * N_BRANCH + (N_V + 1))
                    pe.wait_ge(bias_ready, 1)
                    if t > 0:
                        pe.wait_ge(branch_in, g * 2 * GT + 2 * t)
                    for h in range(HEADS):
                        kv, b = h // WB, h % WB
                        rows = slice(kv * HD, (kv + 1) * HD)
                        last = pe.matmul(logits[:, h, :], qT[rows, b, t * P:(t + 1) * P], kT[rows, t * P:(t + 2) * P],
                                         start=True, stop=True)
                        if h == 0:
                            release(last)
                    last.then_inc(logits_done, 1)
                    for c in range(GATES_PER_TILE * t, GATES_PER_TILE * (t + 1)):
                        rows_of_weights(N_GATE + c, 2 + c // SLOTS, c % SLOTS)
                    pe.wait_ge(probs_ready, g * GT + t + 1)
                    for h in range(HEADS):
                        last = pe.transpose(ptT[:, h, :], probs[:, h * P:(h + 1) * P], ident)
                        if h == 0:
                            release(last)
                    last.then_inc(pt_done, 1)
                    pe.wait_ge(vln_ready, g * GT + t + 1)
                    for q in range(HEADS):
                        last = pe.matmul(sg[(q % 2) * HD:(q % 2 + 1) * HD, q // 2, :], gv[:, t, q * HD:(q + 1) * HD],
                                         par[:, C_WS + q * P:C_WS + (q + 1) * P], start=True, stop=True)
                    last.then_inc(sg_done, 1)
                    pe.wait_ge(pt_masked, g * GT + t + 1)
                    for h in range(HEADS):
                        kv, b = h // WB, h % WB
                        cols = slice(kv * HD, (kv + 1) * HD)
                        pe.matmul(pv[cols, b, :], vtok[:, t, cols], pt_prev[:, h, :], start=True, stop=False)
                        last = pe.matmul(pv[cols, b, :], vtok[:, t + 1, cols], pt_own[:, h, :], start=False, stop=True)
                    last.then_inc(pv_done, 1)

                pe.wait_ge(branch_in, g * 2 * GT + 2 * GT)
                for m in range(KO):
                    chunk_in(4, m)
                    w = wring[:, m, :].rearrange("p (r k m) -> p r k m", r=2, k=WB)
                    for br, src in enumerate((attnT, gmlpT)):
                        n = N_BRANCH + 2 * m + br
                        bank_free(n)
                        for k in range(WB):
                            last = pe.matmul(bank[:, n % BANKS, :], w[:, br, k, :], src[:, k, :],
                                             start=(k == 0), stop=(k == WB - 1))
                            if br == 0 and k == 0:
                                release(last)
                        last.then_inc(product_done, 1)
                    used.append(m)
                pe.wait_ge(merged_ready, g * KO + KO)
                for half in range(2):
                    for c in range(4):
                        s = 4 * half + c
                        chunk_in(5, s)
                        w = wring[:, s, :].rearrange("p (k m) -> p k m", k=2)
                        for t in range(GT):
                            n = N_OUT + half * GT + t
                            if c == 0:
                                bank_free(n)
                            for k in range(2):
                                last = pe.matmul(bank[:, n % BANKS, :], gates[:, 2 * c + k, t * P:(t + 1) * P], w[:, k, :],
                                                 start=(c == 0 and k == 0), stop=(c == 3 and k == 1))
                                if t == 0 and k == 0:
                                    release(last)
                            if c == 3:
                                last.then_inc(product_done, 1)
                        used.append(s)
                pe.wait_ge(product_done, g * N_ALL + N_ALL)
                pe.sem_inc(w_free[used.pop()], 1)

        @block.scalar
        def _(act):
            chain = Chain(act, act_chain)
            act.wait_ge(consts_set, 1)
            with act.Fori(0, GROUPS) as g:
                def product(n):
                    act.wait_ge(product_done, g * N_ALL + (n + 1))
                    return bank[:, n % BANKS, :]

                act.wait_ge(x_loaded, 16 * g + 16)
                for t in range(GT):
                    chain.mark(act.activation(hn[:, t, :], x[:, t, :], ACT.Square, accum_out=ss[:, t:t + 1]))
                chain.wait()
                act.activation(rms[:], ss[:], ACT.Sqrt, bias=eps[:, 0:1], scale=1.0 / D).then_inc(rms_ready, 1)
                for k in range(KO):
                    act.activation(hT[:, k, :], product(N_HT + k), ACT.Copy,
                                   scale=par[:, C_MIXW + k:C_MIXW + k + 1]).then_inc(act_taken, 1)
                for b in range(WB):
                    act.activation(qT[:, b, :], product(N_Q + b), ACT.Copy, scale=HD ** -0.5).then_inc(act_taken, 1)
                act.wait_ge(carry_ready, g + 1)
                act.activation(kT[:, P:], product(N_K), ACT.Copy).then_inc(act_taken, 1)
                act.activation(vtok[:, 1:, :], product(N_V).rearrange("p (t m) -> p t m", t=GT),
                               ACT.Copy).then_inc(act_taken, 1)
                for b in range(WB):
                    act.activation(guT[:, b, :], product(N_GU + b), ACT.Gelu_apprx_tanh).then_inc(act_taken, 1)
                for t in range(GT):
                    act.activation(gv[:, t, :], product(N_GV + t), ACT.Gelu_apprx_tanh).then_inc(act_taken, 1)
                act.wait_ge(ln_var, g + 1)
                act.activation(ln_std[:], mv[:, :, 1], ACT.Sqrt, bias=eps[:, 0:1]).then_inc(ln_std_ready, 1)
                for t in range(GT):
                    for c in range(GATES_PER_TILE):
                        if c == GATES_PER_TILE // 2:
                            act.wait_ge(shifted_ready, g * GT + t + 1)
                            act.activation(probs[:], probs[:], ACT.Exp).then_inc(exp_done, 1)
                        n = N_GATE + GATES_PER_TILE * t + c
                        act.activation(gates[:, n - N_GATE, :], product(n), ACT.Sigmoid).then_inc(act_taken, 1)
                chain.restart()

        @block.vector
        def _(dve):
            chain = Chain(dve, dve_chain)
            step = chain.step
            dve.memset(eps[:], EPS).then_inc(consts_set, 1)
            chain.mark(dve.memset(kT[:, 0:P], 0.0))
            chain.mark(dve.memset(bias_first[:], NEG_INF))
            dve.memset(vtok[:, 0, :], 0.0).then_inc(carry_ready, 1)
            dve.wait_ge(params_in, 16)
            ws = par[:, C_WS:C_WS + HEADS * P].rearrange("p (g t) -> p g t", g=HEADS)
            own01 = par[:, C_OWN01:C_OWN01 + P].unsqueeze(1).to_broadcast([P, HEADS, P])
            prev01 = par[:, C_PREV01:C_PREV01 + P].unsqueeze(1).to_broadcast([P, HEADS, P])
            chain.mark(dve.tensor_tensor(ws, ws, own01, ALU.mult))
            dve.wait_ge(rel_done, 1)
            rel = lflat[:, 0:HEADS * P].rearrange("p (j h) -> p h j", j=P)
            chain.mark(dve.tensor_tensor(bias_own[:], rel, par[:, C_OWNNEG:C_OWNNEG + P].unsqueeze(1).to_broadcast([P, HEADS, P]), ALU.add))
            dve.tensor_tensor(bias_prev[:], rel, par[:, C_PREVNEG:C_PREVNEG + P].unsqueeze(1).to_broadcast([P, HEADS, P]),
                              ALU.add).then_inc(bias_ready, 1)
            dve.wait_ge(bias_ready, 1)
            chain.wait()
            chain.restart()

            lnw = par[:, C_LNW:C_LNW + WIDTH]
            lnb = par[:, C_LNB:C_LNB + WIDTH]
            bs = par[:, C_BS:C_BS + WB * P].rearrange("p (b t) -> p b t", b=WB)
            sinks = par[:, C_SINK:C_SINK + HEADS]
            pm = probs[:, 0:HEADS * P].rearrange("p (h j) -> p h j", h=HEADS)
            psink = probs[:, HEADS * P:]

            def over_keys(a):
                return a.unsqueeze(2).to_broadcast([P, HEADS, P])

            with dve.Fori(0, GROUPS) as g:
                dve.wait_ge(rms_ready, g + 1)
                step(dve.reciprocal(rstd[:], rms[:]))
                for t in range(GT):
                    dve.tensor_scalar(hn[:, t, :], x[:, t, :], rstd[:, t:t + 1], None, ALU.mult).then_inc(hn_ready, 1)

                for t in range(GT):
                    dve.wait_ge(act_taken, g * N_BRANCH + (N_GV + t + 1))
                    chain.mark(dve.bn_stats(stats[:, t, :], gv[:, t, :]))
                chain.wait()
                for t in range(GT):
                    last = dve.bn_aggr(mv[:, t, :], stats[:, t, :])
                last.then_inc(ln_var, 1)
                dve.wait_ge(ln_std_ready, g + 1)
                step(dve.reciprocal(ln_rstd[:], ln_std[:]))
                for t in range(GT):
                    step(dve.tensor_scalar(gv[:, t, :], gv[:, t, :], mv[:, t, 0:1], ln_rstd[:, t:t + 1],
                                           ALU.subtract, ALU.mult))
                    step(dve.tensor_tensor(gv[:, t, :], gv[:, t, :], lnw, ALU.mult))
                    dve.tensor_tensor(gv[:, t, :], gv[:, t, :], lnb, ALU.add).then_inc(vln_ready, 1)

                for t in range(GT):
                    dve.wait_ge(logits_done, g * GT + t + 1)
                    chain.mark(dve.tensor_tensor(pm, logits[:, :, P:2 * P], bias_own[:], ALU.add))
                    step(dve.tensor_tensor(pt_own[:], logits[:, :, 0:P], (bias_first if t == 0 else bias_prev)[:], ALU.add))
                    step(dve.tensor_tensor(pm, pm, pt_own[:], ALU.max))
                    step(dve.tensor_reduce(top[:], pm, AX.X, ALU.max))
                    step(dve.tensor_tensor(top[:], top[:], sinks, ALU.max))
                    chain.mark(dve.tensor_tensor(psink, sinks, top[:], ALU.subtract))
                    dve.tensor_tensor(pm, pm, over_keys(top[:]), ALU.subtract).then_inc(shifted_ready, 1)
                    dve.wait_ge(exp_done, g * GT + t + 1)
                    step(dve.tensor_reduce(den[:], pm, AX.X, ALU.add))
                    step(dve.tensor_tensor(den[:], den[:], psink, ALU.add))
                    step(dve.reciprocal(rden[:], den[:]))
                    dve.tensor_tensor(pm, pm, over_keys(rden[:]), ALU.mult).then_inc(probs_ready, 1)
                    dve.wait_ge(pt_done, g * GT + t + 1)
                    chain.mark(dve.tensor_tensor(pt_own[:], ptT, own01, ALU.mult))
                    dve.tensor_tensor(pt_prev[:], ptT, prev01, ALU.mult).then_inc(pt_masked, 1)
                    cols = slice(t * P, (t + 1) * P)
                    dve.wait_ge(sg_done, g * GT + t + 1)
                    step(dve.tensor_tensor(gmlpT[:, :, cols], sg, bs, ALU.add))
                    dve.tensor_tensor(gmlpT[:, :, cols], gmlpT[:, :, cols], guT[:, :, cols], ALU.mult).then_inc(branch_in, 1)
                    dve.wait_ge(pv_done, g * GT + t + 1)
                    dve.tensor_copy(attnT[:, :, cols], pv).then_inc(branch_in, 1)

                step(dve.tensor_copy(kT[:, 0:P], kT[:, GROUP:GROUP + P]))
                step(dve.tensor_copy(bias_first[:], bias_prev[:]))
                dve.tensor_copy(vtok[:, 0, :], vtok[:, GT, :]).then_inc(carry_ready, 1)

                dve.wait_ge(act_taken, g * N_BRANCH + N_BRANCH)
                for m in range(KO):
                    for br in range(2):
                        n = N_BRANCH + 2 * m + br
                        dve.wait_ge(product_done, g * N_ALL + (n + 1))
                        gate = gates[:, br * KO + m, :]
                        dve.tensor_tensor(gate, gate, bank[:, n % BANKS, :], ALU.mult).then_inc(dve_taken, 1)
                    dve.wait_ge(dve_taken, g * (N_ALL - N_BRANCH) + (2 * m + 2))
                    dve.tensor_tensor(gates[:, m, :], gates[:, m, :], gates[:, KO + m, :], ALU.add).then_inc(merged_ready, 1)
                for n in range(N_OUT, N_ALL):
                    half, t = divmod(n - N_OUT, GT)
                    dve.wait_ge(product_done, g * N_ALL + (n + 1))
                    xs = x[:, t, half * GROUP:(half + 1) * GROUP]
                    dve.tensor_tensor(xs, xs, bank[:, n % BANKS, :], ALU.add).then_inc(dve_taken, 1)
                dve.wait_ge(dve_taken, g * (N_ALL - N_BRANCH) + (N_ALL - N_BRANCH))
                dve.sem_inc(x2_ready, 1)
                chain.restart()


def expert_block(nc, x2, experts, w_query, exp_params, out):
    with ExitStack() as ctx:
        def sb(name, shape, dt=F32):
            return ctx.enter_context(nc.sbuf_tensor(name, shape, dt))

        def sem(name):
            return ctx.enter_context(nc.semaphore(name))

        wq = sb("wq", [P, PH, KO, 2 * NKEYS])
        rows = sb("rows", [P, RING, 2 * D])
        par = sb("epar", [P, EXP_COLS])
        xt = sb("xt", [P, D])
        hnext = sb("hnext", [P, D])
        hcur = sb("hcur", [P, D])
        h2T = sb("h2T", [P, KO, P])
        x3 = sb("x3", [P, D])
        qtok = sb("qtok", [P, 2 * P])
        qhT = sb("qhT", [P, 2, P])
        scores = sb("scores", [P, 2, NKEYS])
        rest = sb("rest", [P, 2, NKEYS])
        val = sb("val", [P, 2, TOPK])
        ind = sb("ind", [P, 2, TOPK], U32)
        cand = sb("cand", [P, TOPK, TOPK])
        cand_rest = sb("cand_rest", [P, TOPK, TOPK])
        best = sb("best", [P, TOPK])
        pos = sb("pos", [P, TOPK], U32)
        digits = sb("digits", [P, 2, TOPK], U32)
        onehot = sb("onehot", [P, 2, TOPK, TOPK])
        picked = sb("picked", [P, 2, TOPK])
        index = sb("index", [P, 2, TOPK], U32)
        negtop = sb("negtop", [P, 1])
        expo = sb("expo", [P, TOPK])
        esum = sb("esum", [P, 1])
        resum = sb("resum", [P, 1])
        gate = sb("gate", [P, 2, TOPK])
        dots = sb("dots", [P, 2, TOPK])
        gelu = sb("gelu", [P, 2, TOPK])
        diag = sb("diag", [P, RING, P])
        ss = sb("ess", [P, 1])
        rms = sb("erms", [P, 1])
        rstd = sb("erstd", [P, 1])
        ss3 = sb("ss3", [P, 1])
        rms3 = sb("rms3", [P, 1])
        rstd3 = sb("rstd3", [P, 1])
        eps = sb("eeps", [P, 1])

        y = ctx.enter_context(nc.psum_tensor("y", [P, 2, GROUP], F32))
        turned = ctx.enter_context(nc.psum_tensor("turned", [P, KO, P], F32))
        query = ctx.enter_context(nc.psum_tensor("query", [P, 4 * P], F32))
        match = ctx.enter_context(nc.psum_tensor("match", [P, 4, NKEYS], F32))

        ident = par[:, E_IDENT:E_IDENT + P]

        params_in = sem("expert_params_in")
        wq_in = sem("wq_in")
        consts_set = sem("expert_consts_set")
        xt_loaded = sem("xt_loaded")
        xt_free = sem("xt_free")
        xt_claimed = sem("xt_claimed")
        rms_ready = sem("tile_rms_ready")
        hnext_ready = sem("hnext_ready")
        turned_done = sem("turned_done")
        h2T_ready = sem("h2T_ready")
        query_done = sem("query_done")
        query_out = sem("query_out")
        qturn_done = sem("qturn_done")
        qhT_ready = sem("qhT_ready")
        match_done = sem("match_done")
        scores_ready = sem("scores_ready")
        scores_seen = sem("scores_seen")
        scores_free = sem("scores_free")
        best_ready = sem("best_ready")
        expo_ready = sem("expo_ready")
        index_ready = sem("index_ready")
        row_landed = [sem(f"row_landed{s}") for s in range(RING)]
        row_free = sem("row_free")
        slot_claimed = sem("slot_claimed")
        dots_ready = sem("dots_ready")
        gelu_ready = sem("gelu_ready")
        diag_ready = sem("diag_ready")
        y_free = sem("y_free")
        rms3_ready = sem("rms3_ready")
        x3_free = sem("x3_free")
        x3_ready = sem("x3_ready")
        out_stored = sem("out_stored")
        dve_chain = sem("expert_dve_chain")
        act_chain = sem("expert_act_chain")

        block = ctx.enter_context(nc.Block())


        @block.sync
        def _(sp):
            sp.dma_start(par[:], exp_params).then_inc(params_in, 16)
            sp.dma_start(xt[:], x2[0]).then_inc(xt_loaded, 16)
            sp.dma_start(wq[:], w_query).then_inc(wq_in, 16)
            sp.sem_inc(x3_free, 1)
            with sp.Fori(0, TILES) as t:
                following = (t + 1) & (TILES - 1)
                sp.wait_ge(xt_free, t + 1)
                sp.sem_inc(xt_claimed, 1)
                sp.dma_start(xt[:], x2[bass.ds(following, 1)].rearrange("t p d -> (t p) d")).then_inc(xt_loaded, 16)
                sp.wait_ge(x3_ready, t + 1)
                sp.dma_start(out[bass.ds(t, 1)].rearrange("t p d -> (t p) d"), x3[:]).then_inc(out_stored, 16)
                sp.wait_ge(out_stored, 16 * t + 16)
                sp.sem_inc(x3_free, 1)
            sp.wait_ge(out_stored, 16 * TILES)

        @block.gpsimd
        def _(pool):
            with pool.Fori(0, TILES * PH // 2) as pair:
                for j in range(2):
                    i = pair * 2 + j
                    pool.wait_ge(index_ready, i + 1)
                    for k in range(TOPK):
                        s = k % RING
                        pool.wait_ge(row_free, i * TOPK + (k + 1))
                        pool.sem_inc(slot_claimed, 1)
                        pool.indirect_dma_start(
                            out=rows[:, s, :], out_offset=None, in_=experts,
                            in_offset=bass.IndirectOffsetOnAxis(ap=index[:, j, k:k + 1], axis=0),
                        ).then_inc(row_landed[s], 16)

        @block.tensor
        def _(pe):
            pe.sem_inc(row_free, RING)
            pe.wait_ge(params_in, 16)

            def turn(t):
                pe.wait_ge(hnext_ready, t + 1)
                for k in range(KO):
                    last = pe.transpose(turned[:, k, :], hnext[:, k * P:(k + 1) * P], ident)
                last.then_inc(turned_done, 1)

            def score(i, h):
                for k in range(KO):
                    w = wq[:, bass.ds(h, 1), k, :].rearrange("p h m -> p (h m)")
                    last = pe.matmul(query[:, 0:2 * P], h2T[:, k, :], w, start=(k == 0), stop=(k == KO - 1))
                last.then_inc(query_done, 1)
                pe.wait_ge(query_out, i + 1)
                for half in range(2):
                    last = pe.transpose(query[:, (2 + half) * P:(3 + half) * P], qtok[:, half * P:(half + 1) * P], ident)
                last.then_inc(qturn_done, 1)
                pe.wait_ge(qhT_ready, i + 1)
                for half in range(2):
                    keys = par[:, E_KEYS + half * NKEYS:E_KEYS + (half + 1) * NKEYS]
                    last = pe.matmul(match[:, half, :], qhT[:, half, :], keys, start=True, stop=True)
                last.then_inc(match_done, 1)

            def add_rows(i, slots):
                for k in slots:
                    s = k % RING
                    pe.wait_ge(diag_ready, i * TOPK + (k + 1))
                    for c in range(2):
                        last = pe.matmul(y[:, c, :], diag[:, s, :], rows[:, s, D + c * GROUP:D + (c + 1) * GROUP],
                                         start=False, stop=False, skip_group_check=True)
                    last.then_inc(row_free, 1)

            early, late = range(3 * BATCH), range(3 * BATCH, TOPK)
            turn(0)
            pe.wait_ge(h2T_ready, 1)
            pe.wait_ge(wq_in, 16)
            score(0, 0)
            pe.wait_ge(scores_ready, 1)
            score(1, 1)
            with pe.Fori(0, TILES) as t:
                pe.wait_ge(y_free, t + 1)
                pe.wait_ge(xt_loaded, 16 * t + 16)
                for c in range(2):
                    last = pe.matmul(y[:, c, :], ident, xt[:, c * GROUP:(c + 1) * GROUP], start=True, stop=True)
                last.then_inc(xt_free, 1)
                with pe.Fori(0, PH - 2) as h:
                    add_rows(t * PH + h, early)
                    score(t * PH + h + 2, h + 2)
                    add_rows(t * PH + h, late)
                add_rows(t * PH + (PH - 2), early)
                turn(t + 1)
                pe.wait_ge(h2T_ready, t + 2)
                score(t * PH + PH, 0)
                add_rows(t * PH + (PH - 2), late)
                add_rows(t * PH + (PH - 1), early)
                score(t * PH + (PH + 1), 1)
                add_rows(t * PH + (PH - 1), late)

        @block.scalar
        def _(act):
            chain = Chain(act, act_chain)
            act.wait_ge(consts_set, 1)
            squares = turned[:].rearrange("p k m -> p (k m)")

            def norm_in(t):
                act.wait_ge(xt_loaded, 16 * t + 16)
                chain.step(act.activation(squares, xt[:], ACT.Square, accum_out=ss[:]))
                act.activation(rms[:], ss[:], ACT.Sqrt, bias=eps[:, 0:1], scale=1.0 / D).then_inc(rms_ready, 1)

            def take_turned(t):
                act.wait_ge(turned_done, t + 1)
                act.activation(h2T[:], turned[:], ACT.Copy).then_inc(h2T_ready, 1)

            def score(i):
                act.wait_ge(query_done, i + 1)
                act.activation(qtok[:], query[:, 0:2 * P], ACT.Copy).then_inc(query_out, 1)
                act.wait_ge(qturn_done, i + 1)
                act.activation(qhT[:].rearrange("p h m -> p (h m)"), query[:, 2 * P:4 * P], ACT.Copy).then_inc(qhT_ready, 1)
                act.wait_ge(match_done, i + 1)
                act.wait_ge(scores_free, i + 1)
                act.activation(scores[:], match[:, 0:2, :], ACT.Copy).then_inc(scores_ready, 1)

            def numerators(i):
                act.wait_ge(best_ready, i + 1)
                act.activation(expo[:], best[:], ACT.Exp, bias=negtop[:, 0:1], accum_out=esum[:]).then_inc(expo_ready, 1)

            def gelus(i, j, batches):
                for b in batches:
                    cols = slice(b * BATCH, (b + 1) * BATCH)
                    act.wait_ge(dots_ready, i * BATCHES + (b + 1))
                    act.activation(gelu[:, j, cols], dots[:, j, cols], ACT.Gelu_apprx_tanh).then_inc(gelu_ready, 1)

            early, late = range(BATCHES // 2), range(BATCHES // 2, BATCHES)

            def head(i, j):
                gelus(i, j, early)
                numerators(i + 1)
                score(i + 2)
                gelus(i, j, late)

            norm_in(0)
            take_turned(0)
            score(0)
            numerators(0)
            score(1)
            with act.Fori(0, TILES) as t:
                chain.restart()
                with act.Fori(0, (PH - 2) // 2) as pair:
                    for j in range(2):
                        head(t * PH + pair * 2 + j, j)
                norm_in(t + 1)
                gelus(t * PH + (PH - 2), 0, early)
                numerators(t * PH + (PH - 1))
                take_turned(t + 1)
                score(t * PH + PH)
                gelus(t * PH + (PH - 2), 0, late)
                head(t * PH + (PH - 1), 1)
                act.wait_ge(row_free, t * (PH * TOPK) + (PH * TOPK + RING))
                act.wait_ge(x3_free, t + 1)
                act.activation(x3[:], y[:].rearrange("p c m -> p (c m)"), ACT.Copy).then_inc(y_free, 1)
                act.wait_ge(y_free, t + 2)
                chain.step(act.activation(squares, x3[:], ACT.Square, accum_out=ss3[:]))
                act.activation(rms3[:], ss3[:], ACT.Sqrt, bias=eps[:, 0:1], scale=1.0 / D).then_inc(rms3_ready, 1)

        @block.vector
        def _(dve):
            chain = Chain(dve, dve_chain)
            mark, step = chain.mark, chain.step
            dve.memset(eps[:], EPS).then_inc(consts_set, 1)
            dve.sem_inc(y_free, 1)
            dve.sem_inc(scores_free, 1)
            dve.wait_ge(params_in, 16)
            iota = par[:, E_IOTA:E_IOTA + TOPK]

            def norm_in(t):
                dve.wait_ge(rms_ready, t + 1)
                step(dve.reciprocal(rstd[:], rms[:]))
                step(dve.scalar_tensor_tensor(out=hnext[:], in0=xt[:], scalar=rstd[:, 0:1], in1=par[:, E_FFNW:E_FFNW + D],
                                              op0=ALU.mult, op1=ALU.mult))
                dve.sem_inc(hnext_ready, 1)

            def top(values, spare_values, found, places, sets):
                for c in range(sets):
                    mark(dve.max(found[c][:, 0:8], values[c]))
                chain.wait()
                for c in range(sets):
                    mark(dve.max_index(places[c][:, 0:8], found[c][:, 0:8], values[c]))
                    mark(dve.match_replace(spare_values[c], found[c][:, 0:8], values[c], LOWEST))
                chain.wait()
                for c in range(sets):
                    mark(dve.max(found[c][:, 8:16], spare_values[c]))
                chain.wait()
                for c in range(sets):
                    mark(dve.max_index(places[c][:, 8:16], found[c][:, 8:16], spare_values[c]))
                chain.wait()

            def best_of_sets(i):
                dve.wait_ge(scores_ready, i + 1)
                dve.sem_inc(scores_seen, 1)
                top([scores[:, c, :] for c in range(2)], [rest[:, c, :] for c in range(2)],
                    [val[:, c, :] for c in range(2)], [ind[:, c, :] for c in range(2)], 2)
                dve.sem_inc(scores_free, 1)

            def best_of_sums():
                step(dve.tensor_tensor(cand[:], val[:, 0, :].unsqueeze(2).to_broadcast([P, TOPK, TOPK]),
                                       val[:, 1, :].unsqueeze(1).to_broadcast([P, TOPK, TOPK]), ALU.add))
                top([cand[:].rearrange("p a b -> p (a b)")], [cand_rest[:].rearrange("p a b -> p (a b)")],
                    [best[:]], [pos[:]], 1)
                step(dve.tensor_scalar(negtop[:], best[:, 0:1], -1.0, None, ALU.mult))
                dve.sem_inc(best_ready, 1)

            def indices(j):
                mark(dve.tensor_scalar(digits[:, 0, :], pos[:], 4, None, ALU.logical_shift_right))
                step(dve.tensor_scalar(digits[:, 1, :], pos[:], TOPK - 1, None, ALU.bitwise_and))
                step(dve.tensor_tensor(onehot[:].rearrange("p c k m -> p (c k) m"),
                                       digits[:].rearrange("p c k -> p (c k)").unsqueeze(2).to_broadcast([P, 2 * TOPK, TOPK]),
                                       iota.unsqueeze(1).to_broadcast([P, 2 * TOPK, TOPK]), ALU.is_equal))
                step(dve.tensor_tensor(onehot[:], onehot[:], ind[:].unsqueeze(2).to_broadcast([P, 2, TOPK, TOPK]), ALU.mult))
                step(dve.tensor_reduce(picked[:].rearrange("p c k -> p (c k)"), onehot[:].rearrange("p c k m -> p (c k) m"),
                                       AX.X, ALU.add))
                dve.scalar_tensor_tensor(out=index[:, j, :], in0=picked[:, 0, :], scalar=float(NKEYS), in1=picked[:, 1, :],
                                         op0=ALU.mult, op1=ALU.add).then_inc(index_ready, 1)

            def normalise(i, j):
                dve.wait_ge(expo_ready, i + 1)
                step(dve.reciprocal(resum[:], esum[:]))
                step(dve.tensor_scalar(gate[:, j, :], expo[:], resum[:, 0:1], None, ALU.mult))

            def diagonals(i, j, b):
                dve.wait_ge(gelu_ready, i * BATCHES + (b + 1))
                for k in range(b * BATCH, (b + 1) * BATCH):
                    dve.tensor_scalar(diag[:, k % RING, :], ident, gelu[:, j, k:k + 1], gate[:, j, k:k + 1],
                                      ALU.mult, ALU.mult).then_inc(diag_ready, 1)

            def head(i, j):
                for b in range(BATCHES):
                    for k in range(b * BATCH, (b + 1) * BATCH):
                        dve.wait_ge(row_landed[k % RING], 16 * (TOPK // RING) * i + 16 * (k // RING + 1))
                        u = rows[:, k % RING, 0:D]
                        last = dve.tensor_tensor_reduce(out=u, in0=u, in1=hcur[:], scale=1.0,
                                                        scalar=0.0, op0=ALU.mult, op1=ALU.add, accum_out=dots[:, j, k:k + 1])
                    last.then_inc(dots_ready, 1)
                    if b > 0:
                        diagonals(i, j, b - 1)
                    if b == 0:
                        best_of_sets(i + 1)
                    if b == 1:
                        best_of_sums()
                    if b == 2:
                        indices(1 - j)
                    if b == BATCHES - 2:
                        normalise(i + 1, 1 - j)
                diagonals(i, j, BATCHES - 1)

            norm_in(0)
            best_of_sets(0)
            best_of_sums()
            indices(0)
            normalise(0, 0)
            step(dve.tensor_copy(hcur[:], hnext[:]))
            with dve.Fori(0, TILES) as t:
                with dve.Fori(0, (PH - 2) // 2) as pair:
                    chain.restart()
                    for j in range(2):
                        head(t * PH + pair * 2 + j, j)
                chain.restart()
                norm_in(t + 1)
                head(t * PH + (PH - 2), 0)
                head(t * PH + (PH - 1), 1)
                step(dve.tensor_copy(hcur[:], hnext[:]))
                dve.wait_ge(rms3_ready, t + 1)
                step(dve.reciprocal(rstd3[:], rms3[:]))
                dve.scalar_tensor_tensor(out=x3[:], in0=x3[:], scalar=rstd3[:, 0:1], in1=par[:, E_FINW:E_FINW + D],
                                         op0=ALU.mult, op1=ALU.mult).then_inc(x3_ready, 1)
                chain.restart()



def distance_buckets():
    n = np.arange(P)
    exact = BUCKETS // 2
    large = exact + (np.log(np.maximum(n, 1) / exact) / np.log(MAX_DISTANCE / exact) * (BUCKETS - exact)).astype(np.int32)
    return np.where(n < exact, n, np.minimum(large, BUCKETS - 1))


def mixer_params(a):
    par = np.zeros((P, MIX_COLS), np.float32)
    i = np.arange(P)
    par[:, C_MIXW:C_SINK] = a["mix_norm_w"][0].reshape(KO, P).T
    par[:, C_SINK:C_LNW] = a["attn_sinks"][0]
    par[:, C_LNW:C_LNB] = a["gmlp_ln_w"][0]
    par[:, C_LNB:C_BS] = a["gmlp_ln_b"][0]
    par[:, C_BS:C_WS] = np.repeat(a["gmlp_b_s"][0].reshape(WB, 2, P).transpose(1, 0, 2).reshape(2, WB * P), HD, axis=0)
    par[:, C_WS:C_IDENT] = a["gmlp_w_s"][0].transpose(2, 0, 1).reshape(P, HEADS * P)
    par[:, C_IDENT:C_OWN01] = np.eye(P)
    par[:, C_OWN01:C_PREV01] = i[:, None] <= i[None, :]
    par[:, C_PREV01:C_OWNNEG] = i[:, None] > i[None, :]
    par[:, C_OWNNEG:C_PREVNEG] = np.where(i[None, :] > i[:, None], NEG_INF, 0)
    par[:, C_PREVNEG:C_DIST] = np.where(i[None, :] <= i[:, None], NEG_INF, 0)
    par[:BUCKETS, C_DIST:C_REL] = distance_buckets()[np.arange(2 * P) % P][None] == np.arange(BUCKETS)[:, None]
    par[:BUCKETS, C_REL:] = a["rel_bias"]
    return par


def mixer_weights(a):
    w_in = a["w_in"][0]
    q0, k0, v0, gu0, gv0, g0 = np.cumsum([0, WIDTH, KV_HEADS * HD, KV_HEADS * HD, WIDTH, WIDTH])
    chunks = np.zeros((ROUNDS * SLOTS, P, CHUNK), np.float32)

    def blocks(w):
        return w.reshape(KO, P, -1, P).transpose(2, 1, 0, 3).reshape(-1, P, CHUNK)

    def pairs(w):
        return w.reshape(KO // 2, 2, P, GROUP).transpose(0, 2, 1, 3).reshape(-1, P, CHUNK)

    wq = w_in[:, q0:k0].reshape(D, 2, WB, HD).transpose(0, 2, 1, 3).reshape(D, WIDTH)
    chunks[0:WB] = blocks(wq)
    chunks[WB:WB + 1] = blocks(w_in[:, k0:v0])
    chunks[WB + 1:WB + 2] = blocks(w_in[:, v0:gu0])
    chunks[SLOTS:SLOTS + WB] = blocks(w_in[:, gu0:gv0])
    chunks[SLOTS + WB:2 * SLOTS] = pairs(w_in[:, gv0:g0])
    chunks[2 * SLOTS:4 * SLOTS] = blocks(w_in[:, g0:])
    wa = a["w_branch_attn"][0].reshape(2, WB, HD, D).transpose(1, 0, 2, 3).reshape(WIDTH, D)
    both = np.stack([wa, a["w_branch_gmlp"][0]]).reshape(2, WB, P, KO, P)
    chunks[4 * SLOTS:5 * SLOTS] = both.transpose(3, 2, 0, 1, 4).reshape(KO, P, CHUNK)
    for half in range(2):
        chunks[5 * SLOTS + 4 * half:5 * SLOTS + 4 * half + 4] = pairs(a["w_out"][0][:, half * GROUP:(half + 1) * GROUP])
    return chunks


def expert_params(a):
    par = np.zeros((P, EXP_COLS), np.float32)
    par[:, E_KEYS:E_KEYS + NKEYS] = a["peer_keys_1"][0].T
    par[:, E_KEYS + NKEYS:E_IDENT] = a["peer_keys_2"][0].T
    par[:, E_IDENT:E_FFNW] = np.eye(P)
    par[:, E_FFNW:E_FINW] = a["ffn_norm_w"][0]
    par[:, E_FINW:E_IOTA] = a["final_norm_w"]
    par[:, E_IOTA:] = np.arange(TOPK)
    return par


def kernel(**inputs):
    import concourse.bacc as _bacc
    from concourse.bass_utils import run_bass_kernel_spmd as _run

    a = {k: np.asarray(v) for k, v in inputs.items()}
    arrays = {
        "x": np.ascontiguousarray(a["x"][0].reshape(GROUPS, GT, P, D).transpose(0, 2, 1, 3)),
        "weights": mixer_weights(a),
        "mix_params": mixer_params(a),
        "experts": np.ascontiguousarray(np.concatenate([a["peer_u"][0], a["peer_v"][0]], axis=1)),
        "w_query": np.ascontiguousarray(a["peer_w_q"][0].reshape(KO, P, PH, 2 * NKEYS).transpose(1, 2, 0, 3)),
        "exp_params": expert_params(a),
    }
    nc = _bacc.Bacc("TRN2", target_bir_lowering=False, num_devices=1)
    d = {n: nc.dram_tensor(f"in_{n}", v.shape, F32, kind="ExternalInput").ap() for n, v in arrays.items()}
    x2 = nc.dram_tensor("mixed_x", (TILES, P, D), F32, kind="Internal").ap()
    out = nc.dram_tensor("out", (1, SEQ, D), F32, kind="ExternalOutput").ap()
    mixer_block(nc, d["x"], d["weights"], d["mix_params"], x2)
    expert_block(nc, x2, d["experts"], d["w_query"], d["exp_params"], out[0].rearrange("(t p) d -> t p d", p=P))
    r = _run(nc, [{f"in_{n}": v for n, v in arrays.items()}], core_ids=[0])
    return r.results[0]["out"]
```

```python
from contextlib import ExitStack

import numpy as np

import concourse.bass as bass
from concourse import mybir

ALU = mybir.AluOpType
ACT = mybir.ActivationFunctionType
AX = mybir.AxisListType
F32 = mybir.dt.float32
F32R = mybir.dt.float32r
U32 = mybir.dt.uint32

P = 128
D = 1024
SEQ = 1024
TILES = SEQ // P
KO = D // P
HEADS = 8
KV_HEADS = 2
HD = 64
WIDTH = HEADS * HD
WB = WIDTH // P
BUCKETS = 32
MAX_DISTANCE = 128
EPS = 1e-6
NEG_INF = -1e30

GROUP = 512
GROUPS = SEQ // GROUP
GT = GROUP // P
BANKS = 4

SLOTS = 8
CHUNK = D
STAGES = 4
SPLITS = 2
QKV_CHUNKS = WB + 2
ROUNDS = 5

N_HT = 0
N_Q = N_HT + KO
N_K = N_Q + WB
N_V = N_K + 1
N_GU = N_V + 1
N_GV = N_GU + WB
N_GATE = N_GV + GT
N_BRANCH = N_GATE + 2 * KO
N_ALL = N_BRANCH + 2 * KO
GATES_PER_TILE = 2 * KO // GT
CHUNKS = ROUNDS * SLOTS - (SLOTS - QKV_CHUNKS)

PH = 8
NKEYS = 128
TOPK = 16
RING = 8
BATCH = 2
BATCHES = TOPK // BATCH
LOWEST = -3.0e38

C_MIXW = 0
C_SINK = C_MIXW + D
C_LNW = C_SINK + HEADS
C_LNB = C_LNW + WIDTH
C_BS = C_LNB + WIDTH
C_WS = C_BS + WB * P
C_IDENT = C_WS + HEADS * P
C_OWN01 = C_IDENT + P
C_PREV01 = C_OWN01 + P
C_OWNNEG = C_PREV01 + P
C_PREVNEG = C_OWNNEG + P
C_DIST = C_PREVNEG + P
C_REL = C_DIST + 2 * P
MIX_COLS = C_REL + HEADS
E_KEYS = 0
E_IDENT = E_KEYS + 2 * NKEYS
E_FFNW = E_IDENT + P
E_FINW = E_FFNW + D
E_IOTA = E_FINW + D
EXP_COLS = E_IOTA + TOPK


class Chain:

    def __init__(self, eng, sem):
        self.eng, self.sem, self.n = eng, sem, 0

    def mark(self, ins):
        self.n += 1
        return ins.then_inc(self.sem, 1)

    def wait(self):
        self.eng.wait_ge(self.sem, self.n)

    def step(self, ins):
        self.mark(ins)
        self.wait()

    def restart(self):
        self.eng.sem_clear(self.sem)
        self.n = 0


def mixer_block(nc, x_in, weights, mix_params, merged_out):
    with ExitStack() as ctx:
        def sb(name, shape, dt=F32):
            return ctx.enter_context(nc.sbuf_tensor(name, shape, dt))

        def sem(name):
            return ctx.enter_context(nc.semaphore(name))

        x = sb("x", [P, GT, D])
        hT_high = sb("hT_high", [P, KO, GROUP], F32R)
        hT_low = sb("hT_low", [P, KO, GROUP], F32R)
        qT = sb("qT", [P, WB, GROUP])
        kT = sb("kT", [P, P + GROUP])
        vtok = sb("vtok", [P, GT + 1, P])
        guv = sb("guv", [P, 2 * WB * GROUP])
        guT = guv[:, 0:WB * GROUP].rearrange("p (b t) -> p b t", b=WB)
        gv = guv[:, WB * GROUP:].rearrange("p (t m) -> p t m", t=GT)
        merged = guv[:].rearrange("p (t k m) -> p t k m", t=GT, k=KO)
        gates = sb("gates", [P, 2 * KO, GROUP])
        attnT_high = sb("attnT_high", [P, WB, GROUP], F32R)
        attnT_low = sb("attnT_low", [P, WB, GROUP], F32R)
        gmlpT_high = sb("gmlpT_high", [P, WB, GROUP], F32R)
        gmlpT_low = sb("gmlpT_low", [P, WB, GROUP], F32R)
        stage = sb("stage", [P, STAGES, CHUNK])
        w_high = sb("w_high", [P, SPLITS, CHUNK], F32R)
        w_low = sb("w_low", [P, SPLITS, CHUNK], F32R)
        par = sb("par", [P, MIX_COLS])
        bias_own = sb("bias_own", [P, HEADS, P])
        bias_prev = sb("bias_prev", [P, HEADS, P])
        before_first = sb("before_first", [P, 1])
        probs = sb("probs", [P, HEADS * P + HEADS])
        pt_own = sb("pt_own", [P, HEADS, P])
        pt_prev = probs[:, 0:HEADS * P].rearrange("p (h i) -> p h i", h=HEADS)
        ss = sb("ss", [P, GT])
        rms = sb("rms", [P, GT])
        rstd = sb("rstd", [P, GT])
        top = sb("top", [P, HEADS])
        den = sb("den", [P, HEADS])
        rden = sb("rden", [P, HEADS])
        stats = sb("stats", [P, GT, 6])
        mv = sb("mv", [P, GT, 2])
        ln_std = sb("ln_std", [P, GT])
        ln_rstd = sb("ln_rstd", [P, GT])
        eps = sb("eps", [P, 1])

        bank = ctx.enter_context(nc.psum_tensor("bank", [P, BANKS, GROUP], F32))
        logits = ctx.enter_context(nc.psum_tensor("logits", [P, HEADS, 2 * P], F32))
        lflat = logits[:].rearrange("p h j -> p (h j)")
        ptT = lflat[:, 0:HEADS * P].rearrange("p (h i) -> p h i", h=HEADS)
        pv = lflat[:, HEADS * P:HEADS * P + WB * P].rearrange("p (b i) -> p b i", b=WB)
        sg = lflat[:, HEADS * P + WB * P:HEADS * P + 2 * WB * P].rearrange("p (b i) -> p b i", b=WB)

        ident = par[:, C_IDENT:C_IDENT + P]

        params_in = sem("params_in")
        x_loaded = [sem(f"x_loaded{t}") for t in range(GT)]
        x_claimed = sem("x_claimed")
        stage_loaded = [sem(f"stage_loaded{s}") for s in range(STAGES)]
        high_ready = sem("high_ready")
        split_ready = sem("split_ready")
        split_free = sem("split_free")
        hT_ready = sem("hT_ready")
        consts_set = sem("consts_set")
        rms_ready = sem("rms_ready")
        hn_ready = sem("hn_ready")
        product_done = sem("product_done")
        act_taken = sem("act_taken")
        dve_taken = sem("dve_taken")
        rel_done = sem("rel_done")
        bias_ready = sem("bias_ready")
        carry_ready = sem("carry_ready")
        ln_var = sem("ln_var")
        ln_std_ready = sem("ln_std_ready")
        vln_ready = sem("vln_ready")
        logits_done = sem("logits_done")
        shifted_ready = sem("shifted_ready")
        exp_done = sem("exp_done")
        probs_ready = sem("probs_ready")
        pt_done = sem("pt_done")
        pt_masked = sem("pt_masked")
        pv_done = sem("pv_done")
        sg_done = sem("sg_done")
        branch_in = sem("branch_in")
        merged_ready = sem("merged_ready")
        banks_free = sem("banks_free")
        merged_stored = sem("merged_stored")
        merged_free = sem("merged_free")
        dve_chain = sem("dve_chain")
        act_chain = sem("act_chain")

        block = ctx.enter_context(nc.Block())

        def chunk_number(r, s):
            return r * SLOTS + s - (0 if isinstance(r, int) and r == 0 else SLOTS - QKV_CHUNKS)

        def stage_loads(g, r, s):
            nth = s // STAGES
            if s % STAGES < QKV_CHUNKS - STAGES:
                return g * (2 * ROUNDS) + (r * 2 + nth)
            return g * (2 * ROUNDS - 1) + (r * 2 + nth - (1 if r > 0 else 0))

        @block.sync
        def _(sp):
            for t in range(GT):
                sp.dma_start(x[:, t, :], x_in[t]).then_inc(x_loaded[t], 16)
            sp.dma_start(par[:], mix_params).then_inc(params_in, 16)
            sp.sem_inc(merged_free, 1)

            def stage_free(g, n):
                sp.wait_ge(split_ready, g * CHUNKS + (n + 1))

            with sp.Fori(0, GROUPS) as g:
                for s in range(QKV_CHUNKS):
                    stage_free(g, s)
                    sp.dma_start(stage[:, s % STAGES, :], weights[s]).then_inc(stage_loaded[s % STAGES], 16)
                for s in range(SLOTS):
                    stage_free(g, chunk_number(1, s) + (SLOTS - QKV_CHUNKS if s < QKV_CHUNKS - STAGES else 0))
                    sp.dma_start(stage[:, s % STAGES, :], weights[SLOTS + s]).then_inc(stage_loaded[s % STAGES], 16)
                with sp.Fori(2, ROUNDS - 1) as r:
                    for s in range(SLOTS):
                        chunk = sp.snap(r * SLOTS + s)
                        stage_free(g, chunk_number(r, s))
                        sp.dma_start(stage[:, s % STAGES, :], weights[bass.ds(chunk, 1)].rearrange(
                            "c p d -> (c p) d")).then_inc(stage_loaded[s % STAGES], 16)
                sp.wait_ge(hT_ready, g * (2 * GT) + 2 * GT)
                sp.sem_inc(x_claimed, 1)
                for t in range(GT):
                    sp.dma_start(x[:, t, :], x_in[bass.ds(((g + 1) & (GROUPS - 1)) * GT + t, 1)].rearrange(
                        "t p d -> (t p) d")).then_inc(x_loaded[t], 16)
                for s in range(SLOTS):
                    stage_free(g, chunk_number(ROUNDS - 1, s))
                    sp.dma_start(stage[:, s % STAGES, :], weights[(ROUNDS - 1) * SLOTS + s]).then_inc(
                        stage_loaded[s % STAGES], 16)
                first_tile = sp.snap(g * GT)
                sp.wait_ge(merged_ready, g * KO + KO)
                sp.dma_start(merged_out[bass.ds(first_tile, GT)].rearrange("t p d -> p t d"),
                             guv[:].rearrange("p (t d) -> p t d", t=GT)).then_inc(merged_stored, 16)
                sp.wait_ge(merged_stored, 16 * g + 16)
                sp.sem_inc(merged_free, 1)
            for t in range(GT):
                sp.wait_ge(x_loaded[t], 16 * (GROUPS + 1))

        @block.gpsimd
        def _(pool):
            pool.sem_inc(split_ready, STAGES)
            with pool.Fori(0, GROUPS) as g:
                for r in range(ROUNDS):
                    for s in range(QKV_CHUNKS if r == 0 else SLOTS):
                        n = chunk_number(r, s)
                        pool.wait_ge(high_ready, g * CHUNKS + (n + 1))
                        pool.tensor_tensor(w_low[:, n % SPLITS, :], stage[:, s % STAGES, :],
                                           w_high[:, n % SPLITS, :].bitcast(F32), ALU.subtract).then_inc(split_ready, 1)

        @block.tensor
        def _(pe):
            pe.sem_inc(split_free, SPLITS)
            pe.wait_ge(params_in, 16)
            rel = lflat[:, 0:HEADS * P].rearrange("p (j h) -> p j h", j=P)
            for j in range(P):
                last = pe.matmul(rel[:, j, :], par[0:BUCKETS, C_DIST + P - j:C_DIST + 2 * P - j],
                                 par[0:BUCKETS, C_REL:C_REL + HEADS], start=True, stop=True)
            last.then_inc(rel_done, 1)

            with pe.Fori(0, GROUPS) as g:
                def bank_free(n):
                    m = n - BANKS
                    if m >= N_BRANCH:
                        pe.wait_ge(dve_taken, g * (N_ALL - N_BRANCH) + (m - N_BRANCH + 1))
                    elif m >= N_Q:
                        pe.wait_ge(act_taken, g * N_BRANCH + (m + 1))
                    elif m >= 0:
                        pe.wait_ge(hT_ready, g * (2 * GT) + (m + 1))

                def chunk_in(r, s, shape, **dims):
                    n = chunk_number(r, s)
                    pe.wait_ge(split_ready, g * CHUNKS + (n + 1 + STAGES))
                    return [w[:, n % SPLITS, :].rearrange(shape, **dims) for w in (w_high, w_low)]

                used = []

                def release(ins):
                    if used:
                        used.pop()
                        ins.then_inc(split_free, 1)

                def three(out, stationary, moving, start, stop):
                    first = pe.matmul(out, stationary[0], moving[0], start=start, stop=False)
                    pe.matmul(out, stationary[0], moving[1], start=False, stop=False)
                    return first, pe.matmul(out, stationary[1], moving[0], start=False, stop=stop)

                def rows_of_weights(n, r, s):
                    w = chunk_in(r, s, "p (k m) -> p k m", k=KO)
                    bank_free(n)
                    for k in range(KO):
                        first, last = three(bank[:, n % BANKS, :], [a[:, k, :] for a in w],
                                            [hT_high[:, k, :], hT_low[:, k, :]], k == 0, k == KO - 1)
                        if k == 0:
                            release(first)
                    last.then_inc(product_done, 1)
                    used.append(n)

                pe.wait_ge(banks_free, g + 1)
                for t in range(GT):
                    pe.wait_ge(hn_ready, g * GT + t + 1)
                    for half in range(2):
                        n = N_HT + 2 * t + half
                        bank_free(n)
                        for k in range(WB):
                            cols = slice((half * WB + k) * P, (half * WB + k + 1) * P)
                            last = pe.transpose(bank[:, n % BANKS, k * P:(k + 1) * P], x[:, t, cols], ident)
                        last.then_inc(product_done, 1)

                pe.wait_ge(hT_ready, g * (2 * GT) + 2 * GT)
                for b in range(WB + 1):
                    rows_of_weights(N_Q + b, 0, b)

                def tokens(k, t):
                    return [a[:, k, t * P:(t + 1) * P] for a in (hT_high, hT_low)]

                w = chunk_in(0, WB + 1, "p (k m) -> p k m", k=KO)
                bank_free(N_V)
                for t in range(GT):
                    for k in range(KO):
                        first, last = three(bank[:, N_V % BANKS, t * P:(t + 1) * P], tokens(k, t), [a[:, k, :] for a in w],
                                            k == 0, k == KO - 1)
                        if t == 0 and k == 0:
                            release(first)
                last.then_inc(product_done, 1)
                used.append(N_V)
                for b in range(WB):
                    rows_of_weights(N_GU + b, 1, b)
                for c in range(4):
                    w = chunk_in(1, WB + c, "p (k m) -> p k m", k=2)
                    for t in range(GT):
                        if c == 0:
                            bank_free(N_GV + t)
                        for k in range(2):
                            first, last = three(bank[:, (N_GV + t) % BANKS, :], tokens(2 * c + k, t), [a[:, k, :] for a in w],
                                                c == 0 and k == 0, c == 3 and k == 1)
                            if t == 0 and k == 0:
                                release(first)
                        if c == 3:
                            last.then_inc(product_done, 1)
                    used.append(N_GV + c)

                for t in range(GT):
                    pe.wait_ge(act_taken, g * N_BRANCH + (N_V + 1))
                    pe.wait_ge(bias_ready, 1)
                    if t > 0:
                        pe.wait_ge(branch_in, g * 2 * GT + 2 * t)
                    for h in range(HEADS):
                        kv, b = h // WB, h % WB
                        rows = slice(kv * HD, (kv + 1) * HD)
                        last = pe.matmul(logits[:, h, :], qT[rows, b, t * P:(t + 1) * P], kT[rows, t * P:(t + 2) * P],
                                         start=True, stop=True)
                        if h == 0:
                            release(last)
                    last.then_inc(logits_done, 1)
                    for c in range(GATES_PER_TILE * t, GATES_PER_TILE * (t + 1)):
                        rows_of_weights(N_GATE + c, 2 + c // SLOTS, c % SLOTS)
                    pe.wait_ge(probs_ready, g * GT + t + 1)
                    for h in range(HEADS):
                        last = pe.transpose(ptT[:, h, :], probs[:, h * P:(h + 1) * P], ident)
                        if h == 0:
                            release(last)
                    last.then_inc(pt_done, 1)
                    pe.wait_ge(vln_ready, g * GT + t + 1)
                    for q in range(HEADS):
                        last = pe.matmul(sg[(q % 2) * HD:(q % 2 + 1) * HD, q // 2, :], gv[:, t, q * HD:(q + 1) * HD],
                                         par[:, C_WS + q * P:C_WS + (q + 1) * P], start=True, stop=True)
                    last.then_inc(sg_done, 1)
                    pe.wait_ge(pt_masked, g * GT + t + 1)
                    for h in range(HEADS):
                        kv, b = h // WB, h % WB
                        cols = slice(kv * HD, (kv + 1) * HD)
                        pe.matmul(pv[cols, b, :], vtok[:, t, cols], pt_prev[:, h, :], start=True, stop=False)
                        last = pe.matmul(pv[cols, b, :], vtok[:, t + 1, cols], pt_own[:, h, :], start=False, stop=True)
                    last.then_inc(pv_done, 1)

                pe.wait_ge(branch_in, g * 2 * GT + 2 * GT)
                for m in range(KO):
                    w = chunk_in(4, m, "p (b k m) -> p b k m", b=2, k=WB)
                    for br, src in enumerate(((attnT_high, attnT_low), (gmlpT_high, gmlpT_low))):
                        n = N_BRANCH + 2 * m + br
                        bank_free(n)
                        for k in range(WB):
                            first, last = three(bank[:, n % BANKS, :], [a[:, br, k, :] for a in w], [a[:, k, :] for a in src],
                                                k == 0, k == WB - 1)
                            if br == 0 and k == 0:
                                release(first)
                        last.then_inc(product_done, 1)
                    used.append(m)
                pe.wait_ge(product_done, g * N_ALL + N_ALL)
                pe.sem_inc(split_free, 1)

        @block.scalar
        def _(act):
            chain = Chain(act, act_chain)
            act.wait_ge(consts_set, 1)

            squares = lflat[:, HEADS * P:]

            def norm(g, t):
                act.wait_ge(x_loaded[t], 16 * g + 16)
                chain.step(act.activation(squares, x[:, t, :], ACT.Square, accum_out=ss[:, t:t + 1]))
                act.activation(rms[:, t:t + 1], ss[:, t:t + 1], ACT.Sqrt, bias=eps[:, 0:1],
                               scale=1.0 / D).then_inc(rms_ready, 1)

            for t in range(GT):
                norm(0, t)
            with act.Fori(0, GROUPS) as g:
                chain.restart()

                def product(n):
                    act.wait_ge(product_done, g * N_ALL + (n + 1))
                    return bank[:, n % BANKS, :]

                def high(n):
                    if n >= CHUNKS:
                        return
                    r, s = divmod(n if n < QKV_CHUNKS else n + SLOTS - QKV_CHUNKS, SLOTS)
                    act.wait_ge(stage_loaded[s % STAGES], stage_loads(g, r, s) * 16 + 16)
                    act.wait_ge(split_free, g * CHUNKS + (n + 1))
                    act.activation(w_high[:, n % SPLITS, :], stage[:, s % STAGES, :], ACT.Copy).then_inc(high_ready, 1)

                high(0)
                high(1)
                for t in range(GT):
                    for half in range(2):
                        act.activation(hT_high[:, half * WB:(half + 1) * WB, t * P:(t + 1) * P],
                                       product(N_HT + 2 * t + half).rearrange("p (k m) -> p k m", k=WB),
                                       ACT.Copy).then_inc(act_taken, 1)
                for b in range(WB):
                    act.activation(qT[:, b, :], product(N_Q + b), ACT.Copy, scale=HD ** -0.5).then_inc(act_taken, 1)
                    high(b + 2)
                act.wait_ge(carry_ready, g + 1)
                act.activation(kT[:, P:], product(N_K), ACT.Copy).then_inc(act_taken, 1)
                high(WB + 2)
                act.activation(vtok[:, 1:, :], product(N_V).rearrange("p (t m) -> p t m", t=GT),
                               ACT.Copy).then_inc(act_taken, 1)
                high(WB + 3)
                act.wait_ge(merged_free, g + 1)
                for b in range(WB):
                    act.activation(guT[:, b, :], product(N_GU + b), ACT.Gelu_apprx_tanh).then_inc(act_taken, 1)
                    high(QKV_CHUNKS + b + 2)
                for c in range(WB, SLOTS - 1):
                    high(QKV_CHUNKS + c + 2)
                for t in range(GT):
                    act.activation(gv[:, t, :], product(N_GV + t), ACT.Gelu_apprx_tanh).then_inc(act_taken, 1)
                high(QKV_CHUNKS + SLOTS + 1)
                act.wait_ge(ln_var, g + 1)
                act.activation(ln_std[:], mv[:, :, 1], ACT.Sqrt, bias=eps[:, 0:1]).then_inc(ln_std_ready, 1)
                for t in range(GT):
                    for c in range(GATES_PER_TILE):
                        if c == GATES_PER_TILE // 2:
                            act.wait_ge(shifted_ready, g * GT + t + 1)
                            act.activation(probs[:], probs[:], ACT.Exp).then_inc(exp_done, 1)
                        n = GATES_PER_TILE * t + c
                        act.activation(gates[:, n, :], product(N_GATE + n), ACT.Sigmoid).then_inc(act_taken, 1)
                        high(chunk_number(2, 0) + n + 2)
                for m in range(KO - 2):
                    high(chunk_number(4, 0) + m + 2)
                    if m == 0:
                        act.wait_ge(branch_in, g * (2 * GT) + 2 * GT)
                    if m < GT:
                        norm(g + 1, m)

        @block.vector
        def _(dve):
            chain = Chain(dve, dve_chain)
            step = chain.step
            dve.memset(eps[:], EPS).then_inc(consts_set, 1)
            dve.sem_inc(banks_free, 1)
            chain.mark(dve.memset(kT[:, 0:P], 0.0))
            chain.mark(dve.memset(before_first[:], NEG_INF))
            dve.memset(vtok[:, 0, :], 0.0).then_inc(carry_ready, 1)
            dve.wait_ge(params_in, 16)
            ws = par[:, C_WS:C_WS + HEADS * P].rearrange("p (g t) -> p g t", g=HEADS)
            own01 = par[:, C_OWN01:C_OWN01 + P].unsqueeze(1).to_broadcast([P, HEADS, P])
            prev01 = par[:, C_PREV01:C_PREV01 + P].unsqueeze(1).to_broadcast([P, HEADS, P])
            chain.mark(dve.tensor_tensor(ws, ws, own01, ALU.mult))
            dve.wait_ge(rel_done, 1)
            rel = lflat[:, 0:HEADS * P].rearrange("p (j h) -> p h j", j=P)
            chain.mark(dve.tensor_tensor(bias_own[:], rel, par[:, C_OWNNEG:C_OWNNEG + P].unsqueeze(1).to_broadcast([P, HEADS, P]), ALU.add))
            dve.tensor_tensor(bias_prev[:], rel, par[:, C_PREVNEG:C_PREVNEG + P].unsqueeze(1).to_broadcast([P, HEADS, P]),
                              ALU.add).then_inc(bias_ready, 1)
            dve.wait_ge(bias_ready, 1)
            chain.wait()
            chain.restart()

            lnw = par[:, C_LNW:C_LNW + WIDTH]
            lnb = par[:, C_LNB:C_LNB + WIDTH]
            bs = par[:, C_BS:C_BS + WB * P].rearrange("p (b t) -> p b t", b=WB)
            sinks = par[:, C_SINK:C_SINK + HEADS]
            pm = probs[:, 0:HEADS * P].rearrange("p (h j) -> p h j", h=HEADS)
            psink = probs[:, HEADS * P:]

            def over_keys(a):
                return a.unsqueeze(2).to_broadcast([P, HEADS, P])

            def norm(g, t):
                dve.wait_ge(rms_ready, g * GT + t + 1)
                step(dve.reciprocal(rstd[:, t:t + 1], rms[:, t:t + 1]))
                dve.scalar_tensor_tensor(out=x[:, t, :], in0=x[:, t, :], scalar=rstd[:, t:t + 1], in1=par[:, C_MIXW:C_MIXW + D],
                                         op0=ALU.mult, op1=ALU.mult).then_inc(hn_ready, 1)

            for t in range(GT):
                norm(0, t)
            chain.restart()
            with dve.Fori(0, GROUPS) as g:
                for n in range(2 * GT):
                    t, half = divmod(n, 2)
                    part = (slice(None), slice(half * WB, (half + 1) * WB), slice(t * P, (t + 1) * P))
                    dve.wait_ge(act_taken, g * N_BRANCH + (N_HT + n + 1))
                    dve.tensor_tensor(hT_low[part], bank[:, (N_HT + n) % BANKS, :].rearrange("p (k m) -> p k m", k=WB),
                                      hT_high[part].bitcast(F32), ALU.subtract).then_inc(hT_ready, 1)
                for t in range(GT):
                    dve.wait_ge(act_taken, g * N_BRANCH + (N_GV + t + 1))
                    chain.mark(dve.bn_stats(stats[:, t, :], gv[:, t, :]))
                chain.wait()
                for t in range(GT):
                    last = dve.bn_aggr(mv[:, t, :], stats[:, t, :])
                last.then_inc(ln_var, 1)
                dve.wait_ge(ln_std_ready, g + 1)
                step(dve.reciprocal(ln_rstd[:], ln_std[:]))
                for t in range(GT):
                    step(dve.tensor_scalar(gv[:, t, :], gv[:, t, :], mv[:, t, 0:1], ln_rstd[:, t:t + 1],
                                           ALU.subtract, ALU.mult))
                    step(dve.tensor_tensor(gv[:, t, :], gv[:, t, :], lnw, ALU.mult))
                    dve.tensor_tensor(gv[:, t, :], gv[:, t, :], lnb, ALU.add).then_inc(vln_ready, 1)

                for t in range(GT):
                    dve.wait_ge(logits_done, g * GT + t + 1)
                    chain.mark(dve.tensor_tensor(pm, logits[:, :, P:2 * P], bias_own[:], ALU.add))
                    if t == 0:
                        step(dve.scalar_tensor_tensor(out=pt_own[:], in0=logits[:, :, 0:P], scalar=before_first[:, 0:1],
                                                      in1=bias_prev[:], op0=ALU.add, op1=ALU.add))
                    else:
                        step(dve.tensor_tensor(pt_own[:], logits[:, :, 0:P], bias_prev[:], ALU.add))
                    step(dve.tensor_tensor(pm, pm, pt_own[:], ALU.max))
                    step(dve.tensor_reduce(top[:], pm, AX.X, ALU.max))
                    step(dve.tensor_tensor(top[:], top[:], sinks, ALU.max))
                    chain.mark(dve.tensor_tensor(psink, sinks, top[:], ALU.subtract))
                    dve.tensor_tensor(pm, pm, over_keys(top[:]), ALU.subtract).then_inc(shifted_ready, 1)
                    dve.wait_ge(exp_done, g * GT + t + 1)
                    step(dve.tensor_reduce(den[:], pm, AX.X, ALU.add))
                    step(dve.tensor_tensor(den[:], den[:], psink, ALU.add))
                    step(dve.reciprocal(rden[:], den[:]))
                    dve.tensor_tensor(pm, pm, over_keys(rden[:]), ALU.mult).then_inc(probs_ready, 1)
                    dve.wait_ge(pt_done, g * GT + t + 1)
                    chain.mark(dve.tensor_tensor(pt_own[:], ptT, own01, ALU.mult))
                    dve.tensor_tensor(pt_prev, ptT, prev01, ALU.mult).then_inc(pt_masked, 1)
                    cols = slice(t * P, (t + 1) * P)
                    dve.wait_ge(sg_done, g * GT + t + 1)
                    gated = gv[:, t, :].rearrange("p (b i) -> p b i", b=WB)
                    step(dve.tensor_tensor(gated, sg, bs, ALU.add))
                    step(dve.tensor_tensor(gated, gated, guT[:, :, cols], ALU.mult))
                    step(dve.tensor_copy(gmlpT_high[:, :, cols], gated))
                    dve.tensor_tensor(gmlpT_low[:, :, cols], gated, gmlpT_high[:, :, cols].bitcast(F32),
                                      ALU.subtract).then_inc(branch_in, 1)
                    dve.wait_ge(pv_done, g * GT + t + 1)
                    step(dve.tensor_copy(attnT_high[:, :, cols], pv))
                    dve.tensor_tensor(attnT_low[:, :, cols], pv, attnT_high[:, :, cols].bitcast(F32),
                                      ALU.subtract).then_inc(branch_in, 1)

                step(dve.tensor_copy(kT[:, 0:P], kT[:, GROUP:GROUP + P]))
                step(dve.memset(before_first[:], 0.0))
                dve.tensor_copy(vtok[:, 0, :], vtok[:, GT, :]).then_inc(carry_ready, 1)

                dve.wait_ge(act_taken, g * N_BRANCH + N_BRANCH)
                for m in range(KO):
                    for br in range(2):
                        n = N_BRANCH + 2 * m + br
                        dve.wait_ge(product_done, g * N_ALL + (n + 1))
                        gate = gates[:, br * KO + m, :]
                        dve.tensor_tensor(gate, gate, bank[:, n % BANKS, :], ALU.mult).then_inc(dve_taken, 1)
                    dve.wait_ge(dve_taken, g * (N_ALL - N_BRANCH) + (2 * m + 2))
                    dve.tensor_tensor(merged[:, :, m, :], gates[:, m, :].rearrange("p (t m) -> p t m", t=GT),
                                      gates[:, KO + m, :].rearrange("p (t m) -> p t m", t=GT), ALU.add).then_inc(merged_ready, 1)
                    if m % 2 == 1:
                        norm(g + 1, m // 2)
                dve.sem_inc(banks_free, 1)
                chain.restart()


def expert_block(nc, x_in, merged_in, w_out, experts, w_query, exp_params, out):
    with ExitStack() as ctx:
        def sb(name, shape, dt=F32):
            return ctx.enter_context(nc.sbuf_tensor(name, shape, dt))

        def sem(name):
            return ctx.enter_context(nc.semaphore(name))

        wout = sb("wout", [P, KO, D])
        mt = sb("mt", [P, KO, P])
        wq = sb("wq", [P, PH, KO, 2 * NKEYS])
        rows = sb("rows", [P, RING, 2 * D])
        par = sb("epar", [P, EXP_COLS])
        xt = sb("xt", [P, D])
        hnext = sb("hnext", [P, D])
        hcur = sb("hcur", [P, D])
        h2T = sb("h2T", [P, KO, P])
        x3 = sb("x3", [P, D])
        qtok = sb("qtok", [P, 2 * P])
        qhT = sb("qhT", [P, 2, P])
        scores = sb("scores", [P, 2, NKEYS])
        rest = sb("rest", [P, 2, NKEYS])
        val = sb("val", [P, 2, TOPK])
        ind = sb("ind", [P, 2, TOPK], U32)
        cand = sb("cand", [P, TOPK, TOPK])
        cand_rest = sb("cand_rest", [P, TOPK, TOPK])
        best = sb("best", [P, TOPK])
        pos = sb("pos", [P, TOPK], U32)
        digits = sb("digits", [P, 2, TOPK], U32)
        onehot = sb("onehot", [P, 2, TOPK, TOPK])
        picked = sb("picked", [P, 2, TOPK])
        index = sb("index", [P, 2, TOPK], U32)
        negtop = sb("negtop", [P, 1])
        expo = sb("expo", [P, TOPK])
        esum = sb("esum", [P, 1])
        resum = sb("resum", [P, 1])
        gate = sb("gate", [P, 2, TOPK])
        dots = sb("dots", [P, 2, TOPK])
        gelu = sb("gelu", [P, 2, TOPK])
        diag = sb("diag", [P, RING, P])
        ss = sb("ess", [P, 1])
        rms = sb("erms", [P, 1])
        rstd = sb("erstd", [P, 1])
        ss3 = sb("ss3", [P, 1])
        rms3 = sb("rms3", [P, 1])
        rstd3 = sb("rstd3", [P, 1])
        eps = sb("eeps", [P, 1])

        y = ctx.enter_context(nc.psum_tensor("y", [P, 2, GROUP], F32))
        turned = ctx.enter_context(nc.psum_tensor("turned", [P, KO, P], F32))
        mixed = ctx.enter_context(nc.psum_tensor("mixed", [P, 2, GROUP], F32))
        query = ctx.enter_context(nc.psum_tensor("query", [P, 4 * P], F32))
        match = ctx.enter_context(nc.psum_tensor("match", [P, 4, NKEYS], F32))

        ident = par[:, E_IDENT:E_IDENT + P]

        params_in = sem("expert_params_in")
        wout_in = [sem(f"wout_in{c}") for c in range(2)]
        wq_first_in = sem("wq_first_in")
        wq_in = sem("wq_in")
        mt_loaded = sem("mt_loaded")
        mixed_done = sem("mixed_done")
        x2_ready = sem("x2_ready")
        consts_set = sem("expert_consts_set")
        xt_loaded = sem("xt_loaded")
        xt_free = sem("xt_free")
        xt_claimed = sem("xt_claimed")
        rms_ready = sem("tile_rms_ready")
        hnext_ready = sem("hnext_ready")
        turned_done = sem("turned_done")
        h2T_ready = sem("h2T_ready")
        query_done = sem("query_done")
        query_out = sem("query_out")
        qturn_done = sem("qturn_done")
        qhT_ready = sem("qhT_ready")
        match_done = sem("match_done")
        scores_ready = sem("scores_ready")
        scores_seen = sem("scores_seen")
        scores_free = sem("scores_free")
        best_ready = sem("best_ready")
        expo_ready = sem("expo_ready")
        index_ready = sem("index_ready")
        row_landed = [sem(f"row_landed{s}") for s in range(RING)]
        row_free = sem("row_free")
        slot_claimed = sem("slot_claimed")
        dots_ready = sem("dots_ready")
        gelu_ready = sem("gelu_ready")
        diag_ready = sem("diag_ready")
        y_free = sem("y_free")
        rms3_ready = sem("rms3_ready")
        x3_free = sem("x3_free")
        x3_ready = sem("x3_ready")
        out_stored = sem("out_stored")
        dve_chain = sem("expert_dve_chain")
        act_chain = sem("expert_act_chain")

        block = ctx.enter_context(nc.Block())


        @block.sync
        def _(sp):
            sp.dma_start(mt[:].rearrange("p k m -> p (k m)"), merged_in[0]).then_inc(mt_loaded, 16)
            for c in range(2):
                cols = slice(c * GROUP, (c + 1) * GROUP)
                sp.dma_start(wout[:, :, cols], w_out[:, :, cols]).then_inc(wout_in[c], 16)
            sp.dma_start(xt[:], x_in[0]).then_inc(xt_loaded, 16)
            sp.dma_start(par[:], exp_params).then_inc(params_in, 16)
            sp.dma_start(wq[:, 0:2], w_query[:, 0:2]).then_inc(wq_first_in, 16)
            sp.dma_start(wq[:, 2:PH], w_query[:, 2:PH]).then_inc(wq_in, 16)
            sp.sem_inc(x3_free, 1)
            with sp.Fori(0, TILES) as t:
                following = (t + 1) & (TILES - 1)
                sp.wait_ge(xt_free, t + 1)
                sp.sem_inc(xt_claimed, 1)
                sp.dma_start(xt[:], x_in[bass.ds(following, 1)].rearrange("t p d -> (t p) d")).then_inc(xt_loaded, 16)
                sp.dma_start(mt[:].rearrange("p k m -> p (k m)"), merged_in[bass.ds(following, 1)].rearrange(
                    "t p d -> (t p) d")).then_inc(mt_loaded, 16)
                sp.wait_ge(x3_ready, t + 1)
                sp.dma_start(out[bass.ds(t, 1)].rearrange("t p d -> (t p) d"), x3[:]).then_inc(out_stored, 16)
                sp.wait_ge(out_stored, 16 * t + 16)
                sp.sem_inc(x3_free, 1)
            sp.wait_ge(out_stored, 16 * TILES)

        @block.gpsimd
        def _(pool):
            with pool.Fori(0, TILES * PH // 2) as pair:
                for j in range(2):
                    i = pair * 2 + j
                    pool.wait_ge(index_ready, i + 1)
                    for k in range(TOPK):
                        s = k % RING
                        pool.wait_ge(row_free, i * TOPK + (k + 1))
                        pool.sem_inc(slot_claimed, 1)
                        pool.indirect_dma_start(
                            out=rows[:, s, :], out_offset=None, in_=experts,
                            in_offset=bass.IndirectOffsetOnAxis(ap=index[:, j, k:k + 1], axis=0),
                        ).then_inc(row_landed[s], 16)

        @block.tensor
        def _(pe):
            pe.sem_inc(row_free, RING)

            def mix(t):
                pe.wait_ge(mt_loaded, 16 * t + 16)
                for c in range(2):
                    if isinstance(t, int):
                        pe.wait_ge(wout_in[c], 16)
                    for k in range(KO):
                        last = pe.matmul(mixed[:, c, :], mt[:, k, :], wout[:, k, c * GROUP:(c + 1) * GROUP],
                                         start=(k == 0), stop=(k == KO - 1))
                last.then_inc(mixed_done, 1)

            def turn(t):
                pe.wait_ge(hnext_ready, t + 1)
                for k in range(KO):
                    last = pe.transpose(turned[:, k, :], hnext[:, k * P:(k + 1) * P], ident)
                last.then_inc(turned_done, 1)

            def score(i, h):
                for k in range(KO):
                    w = wq[:, bass.ds(h, 1), k, :].rearrange("p h m -> p (h m)")
                    last = pe.matmul(query[:, 0:2 * P], h2T[:, k, :], w, start=(k == 0), stop=(k == KO - 1))
                last.then_inc(query_done, 1)
                pe.wait_ge(query_out, i + 1)
                for half in range(2):
                    last = pe.transpose(query[:, (2 + half) * P:(3 + half) * P], qtok[:, half * P:(half + 1) * P], ident)
                last.then_inc(qturn_done, 1)
                pe.wait_ge(qhT_ready, i + 1)
                for half in range(2):
                    keys = par[:, E_KEYS + half * NKEYS:E_KEYS + (half + 1) * NKEYS]
                    last = pe.matmul(match[:, half, :], qhT[:, half, :], keys, start=True, stop=True)
                last.then_inc(match_done, 1)

            def add_rows(i, slots):
                for k in slots:
                    s = k % RING
                    pe.wait_ge(diag_ready, i * TOPK + (k + 1))
                    for c in range(2):
                        last = pe.matmul(y[:, c, :], diag[:, s, :], rows[:, s, D + c * GROUP:D + (c + 1) * GROUP],
                                         start=False, stop=False, skip_group_check=True)
                    last.then_inc(row_free, 1)

            early, late = range(3 * BATCH), range(3 * BATCH, TOPK)
            mix(0)
            pe.wait_ge(params_in, 16)
            turn(0)
            pe.wait_ge(h2T_ready, 1)
            pe.wait_ge(wq_first_in, 16)
            score(0, 0)
            pe.wait_ge(scores_ready, 1)
            score(1, 1)
            pe.wait_ge(wq_in, 16)
            with pe.Fori(0, TILES) as t:
                pe.wait_ge(y_free, t + 1)
                for c in range(2):
                    last = pe.matmul(y[:, c, :], ident, xt[:, c * GROUP:(c + 1) * GROUP], start=True, stop=True)
                last.then_inc(xt_free, 1)
                with pe.Fori(0, PH - 2) as h:
                    add_rows(t * PH + h, early)
                    score(t * PH + h + 2, h + 2)
                    add_rows(t * PH + h, late)
                mix(t + 1)
                add_rows(t * PH + (PH - 2), range(5 * BATCH))
                turn(t + 1)
                pe.wait_ge(h2T_ready, t + 2)
                score(t * PH + PH, 0)
                add_rows(t * PH + (PH - 2), range(5 * BATCH, TOPK))
                add_rows(t * PH + (PH - 1), early)
                score(t * PH + (PH + 1), 1)
                add_rows(t * PH + (PH - 1), late)

        @block.scalar
        def _(act):
            chain = Chain(act, act_chain)
            act.wait_ge(consts_set, 1)
            squares = turned[:].rearrange("p k m -> p (k m)")

            def norm_in(t):
                act.wait_ge(x2_ready, t + 1)
                chain.step(act.activation(squares, xt[:], ACT.Square, accum_out=ss[:]))
                act.activation(rms[:], ss[:], ACT.Sqrt, bias=eps[:, 0:1], scale=1.0 / D).then_inc(rms_ready, 1)

            def take_turned(t):
                act.wait_ge(turned_done, t + 1)
                act.activation(h2T[:], turned[:], ACT.Copy).then_inc(h2T_ready, 1)

            def score(i):
                act.wait_ge(query_done, i + 1)
                act.activation(qtok[:], query[:, 0:2 * P], ACT.Copy).then_inc(query_out, 1)
                act.wait_ge(qturn_done, i + 1)
                act.activation(qhT[:].rearrange("p h m -> p (h m)"), query[:, 2 * P:4 * P], ACT.Copy).then_inc(qhT_ready, 1)
                act.wait_ge(match_done, i + 1)
                act.wait_ge(scores_free, i + 1)
                act.activation(scores[:], match[:, 0:2, :], ACT.Copy).then_inc(scores_ready, 1)

            def numerators(i):
                act.wait_ge(best_ready, i + 1)
                act.activation(expo[:], best[:], ACT.Exp, bias=negtop[:, 0:1], accum_out=esum[:]).then_inc(expo_ready, 1)

            def gelus(i, j, batches):
                for b in batches:
                    cols = slice(b * BATCH, (b + 1) * BATCH)
                    act.wait_ge(dots_ready, i * BATCHES + (b + 1))
                    act.activation(gelu[:, j, cols], dots[:, j, cols], ACT.Gelu_apprx_tanh).then_inc(gelu_ready, 1)

            early, late = range(BATCHES // 2), range(BATCHES // 2, BATCHES)

            def head(i, j):
                gelus(i, j, early)
                numerators(i + 1)
                score(i + 2)
                gelus(i, j, late)

            norm_in(0)
            take_turned(0)
            score(0)
            numerators(0)
            score(1)
            with act.Fori(0, TILES) as t:
                chain.restart()
                with act.Fori(0, (PH - 2) // 2) as pair:
                    for j in range(2):
                        head(t * PH + pair * 2 + j, j)
                gelus(t * PH + (PH - 2), 0, early)
                norm_in(t + 1)
                numerators(t * PH + (PH - 1))
                gelus(t * PH + (PH - 2), 0, late[:2])
                take_turned(t + 1)
                score(t * PH + PH)
                gelus(t * PH + (PH - 2), 0, late[2:])
                head(t * PH + (PH - 1), 1)
                act.wait_ge(row_free, t * (PH * TOPK) + (PH * TOPK + RING))
                act.wait_ge(x3_free, t + 1)
                act.activation(x3[:], y[:].rearrange("p c m -> p (c m)"), ACT.Copy).then_inc(y_free, 1)
                act.wait_ge(y_free, t + 2)
                chain.step(act.activation(squares, x3[:], ACT.Square, accum_out=ss3[:]))
                act.activation(rms3[:], ss3[:], ACT.Sqrt, bias=eps[:, 0:1], scale=1.0 / D).then_inc(rms3_ready, 1)

        @block.vector
        def _(dve):
            chain = Chain(dve, dve_chain)
            mark, step = chain.mark, chain.step
            dve.memset(eps[:], EPS).then_inc(consts_set, 1)
            dve.sem_inc(y_free, 1)
            dve.sem_inc(scores_free, 1)
            dve.wait_ge(params_in, 16)
            iota = par[:, E_IOTA:E_IOTA + TOPK]

            def residual(t):
                dve.wait_ge(xt_loaded, 16 * t + 16)
                dve.wait_ge(mixed_done, t + 1)
                dve.tensor_tensor(xt[:], xt[:], mixed[:].rearrange("p c m -> p (c m)"), ALU.add).then_inc(x2_ready, 1)

            def norm_in(t):
                dve.wait_ge(rms_ready, t + 1)
                step(dve.reciprocal(rstd[:], rms[:]))
                step(dve.scalar_tensor_tensor(out=hnext[:], in0=xt[:], scalar=rstd[:, 0:1], in1=par[:, E_FFNW:E_FFNW + D],
                                              op0=ALU.mult, op1=ALU.mult))
                dve.sem_inc(hnext_ready, 1)

            def top(values, spare_values, found, places, sets):
                for c in range(sets):
                    mark(dve.max(found[c][:, 0:8], values[c]))
                chain.wait()
                for c in range(sets):
                    mark(dve.max_index(places[c][:, 0:8], found[c][:, 0:8], values[c]))
                    mark(dve.match_replace(spare_values[c], found[c][:, 0:8], values[c], LOWEST))
                chain.wait()
                for c in range(sets):
                    mark(dve.max(found[c][:, 8:16], spare_values[c]))
                chain.wait()
                for c in range(sets):
                    mark(dve.max_index(places[c][:, 8:16], found[c][:, 8:16], spare_values[c]))
                chain.wait()

            def best_of_sets(i):
                dve.wait_ge(scores_ready, i + 1)
                dve.sem_inc(scores_seen, 1)
                top([scores[:, c, :] for c in range(2)], [rest[:, c, :] for c in range(2)],
                    [val[:, c, :] for c in range(2)], [ind[:, c, :] for c in range(2)], 2)
                dve.sem_inc(scores_free, 1)

            def best_of_sums():
                step(dve.tensor_tensor(cand[:], val[:, 0, :].unsqueeze(2).to_broadcast([P, TOPK, TOPK]),
                                       val[:, 1, :].unsqueeze(1).to_broadcast([P, TOPK, TOPK]), ALU.add))
                top([cand[:].rearrange("p a b -> p (a b)")], [cand_rest[:].rearrange("p a b -> p (a b)")],
                    [best[:]], [pos[:]], 1)
                step(dve.tensor_scalar(negtop[:], best[:, 0:1], -1.0, None, ALU.mult))
                dve.sem_inc(best_ready, 1)

            def indices(j):
                mark(dve.tensor_scalar(digits[:, 0, :], pos[:], 4, None, ALU.logical_shift_right))
                step(dve.tensor_scalar(digits[:, 1, :], pos[:], TOPK - 1, None, ALU.bitwise_and))
                step(dve.tensor_tensor(onehot[:].rearrange("p c k m -> p (c k) m"),
                                       digits[:].rearrange("p c k -> p (c k)").unsqueeze(2).to_broadcast([P, 2 * TOPK, TOPK]),
                                       iota.unsqueeze(1).to_broadcast([P, 2 * TOPK, TOPK]), ALU.is_equal))
                step(dve.tensor_tensor(onehot[:], onehot[:], ind[:].unsqueeze(2).to_broadcast([P, 2, TOPK, TOPK]), ALU.mult))
                step(dve.tensor_reduce(picked[:].rearrange("p c k -> p (c k)"), onehot[:].rearrange("p c k m -> p (c k) m"),
                                       AX.X, ALU.add))
                dve.scalar_tensor_tensor(out=index[:, j, :], in0=picked[:, 0, :], scalar=float(NKEYS), in1=picked[:, 1, :],
                                         op0=ALU.mult, op1=ALU.add).then_inc(index_ready, 1)

            def normalise(i, j):
                dve.wait_ge(expo_ready, i + 1)
                step(dve.reciprocal(resum[:], esum[:]))
                step(dve.tensor_scalar(gate[:, j, :], expo[:], resum[:, 0:1], None, ALU.mult))

            def diagonals(i, j, b):
                dve.wait_ge(gelu_ready, i * BATCHES + (b + 1))
                for k in range(b * BATCH, (b + 1) * BATCH):
                    dve.tensor_scalar(diag[:, k % RING, :], ident, gelu[:, j, k:k + 1], gate[:, j, k:k + 1],
                                      ALU.mult, ALU.mult).then_inc(diag_ready, 1)

            def head(i, j, following=None):
                for b in range(BATCHES):
                    for k in range(b * BATCH, (b + 1) * BATCH):
                        dve.wait_ge(row_landed[k % RING], 16 * (TOPK // RING) * i + 16 * (k // RING + 1))
                        u = rows[:, k % RING, 0:D]
                        last = dve.tensor_tensor_reduce(out=u, in0=u, in1=hcur[:], scale=1.0,
                                                        scalar=0.0, op0=ALU.mult, op1=ALU.add, accum_out=dots[:, j, k:k + 1])
                    last.then_inc(dots_ready, 1)
                    if b > 0:
                        diagonals(i, j, b - 1)
                    if b == 1:
                        best_of_sets(i + 1)
                    if b == 2:
                        best_of_sums()
                    if b == 3:
                        indices(1 - j)
                    if following is not None and b == 2:
                        residual(following)
                    if following is not None and b == 4:
                        norm_in(following)
                    if b == BATCHES - 2:
                        normalise(i + 1, 1 - j)
                diagonals(i, j, BATCHES - 1)

            residual(0)
            norm_in(0)
            best_of_sets(0)
            best_of_sums()
            indices(0)
            normalise(0, 0)
            step(dve.tensor_copy(hcur[:], hnext[:]))
            with dve.Fori(0, TILES) as t:
                with dve.Fori(0, (PH - 2) // 2) as pair:
                    chain.restart()
                    for j in range(2):
                        head(t * PH + pair * 2 + j, j)
                chain.restart()
                head(t * PH + (PH - 2), 0, following=t + 1)
                head(t * PH + (PH - 1), 1)
                step(dve.tensor_copy(hcur[:], hnext[:]))
                dve.wait_ge(rms3_ready, t + 1)
                step(dve.reciprocal(rstd3[:], rms3[:]))
                dve.scalar_tensor_tensor(out=x3[:], in0=x3[:], scalar=rstd3[:, 0:1], in1=par[:, E_FINW:E_FINW + D],
                                         op0=ALU.mult, op1=ALU.mult).then_inc(x3_ready, 1)
                chain.restart()



def distance_buckets():
    n = np.arange(P)
    exact = BUCKETS // 2
    large = exact + (np.log(np.maximum(n, 1) / exact) / np.log(MAX_DISTANCE / exact) * (BUCKETS - exact)).astype(np.int32)
    return np.where(n < exact, n, np.minimum(large, BUCKETS - 1))


def mixer_params(a):
    par = np.zeros((P, MIX_COLS), np.float32)
    i = np.arange(P)
    par[:, C_MIXW:C_SINK] = a["mix_norm_w"][0]
    par[:, C_SINK:C_LNW] = a["attn_sinks"][0]
    par[:, C_LNW:C_LNB] = a["gmlp_ln_w"][0]
    par[:, C_LNB:C_BS] = a["gmlp_ln_b"][0]
    par[:, C_BS:C_WS] = np.repeat(a["gmlp_b_s"][0].reshape(WB, 2, P).transpose(1, 0, 2).reshape(2, WB * P), HD, axis=0)
    par[:, C_WS:C_IDENT] = a["gmlp_w_s"][0].transpose(2, 0, 1).reshape(P, HEADS * P)
    par[:, C_IDENT:C_OWN01] = np.eye(P)
    par[:, C_OWN01:C_PREV01] = i[:, None] <= i[None, :]
    par[:, C_PREV01:C_OWNNEG] = i[:, None] > i[None, :]
    par[:, C_OWNNEG:C_PREVNEG] = np.where(i[None, :] > i[:, None], NEG_INF, 0)
    par[:, C_PREVNEG:C_DIST] = np.where(i[None, :] <= i[:, None], NEG_INF, 0)
    par[:BUCKETS, C_DIST:C_REL] = distance_buckets()[np.arange(2 * P) % P][None] == np.arange(BUCKETS)[:, None]
    par[:BUCKETS, C_REL:] = a["rel_bias"]
    return par


def mixer_weights(a):
    w_in = a["w_in"][0]
    q0, k0, v0, gu0, gv0, g0 = np.cumsum([0, WIDTH, KV_HEADS * HD, KV_HEADS * HD, WIDTH, WIDTH])
    chunks = np.zeros((ROUNDS * SLOTS, P, CHUNK), np.float32)

    def blocks(w):
        return w.reshape(KO, P, -1, P).transpose(2, 1, 0, 3).reshape(-1, P, CHUNK)

    def pairs(w):
        return w.reshape(KO // 2, 2, P, GROUP).transpose(0, 2, 1, 3).reshape(-1, P, CHUNK)

    wq = w_in[:, q0:k0].reshape(D, 2, WB, HD).transpose(0, 2, 1, 3).reshape(D, WIDTH)
    chunks[0:WB] = blocks(wq)
    chunks[WB:WB + 1] = blocks(w_in[:, k0:v0])
    chunks[WB + 1:WB + 2] = blocks(w_in[:, v0:gu0])
    chunks[SLOTS:SLOTS + WB] = blocks(w_in[:, gu0:gv0])
    chunks[SLOTS + WB:2 * SLOTS] = pairs(w_in[:, gv0:g0])
    chunks[2 * SLOTS:4 * SLOTS] = blocks(w_in[:, g0:])
    wa = a["w_branch_attn"][0].reshape(2, WB, HD, D).transpose(1, 0, 2, 3).reshape(WIDTH, D)
    both = np.stack([wa, a["w_branch_gmlp"][0]]).reshape(2, WB, P, KO, P)
    chunks[4 * SLOTS:5 * SLOTS] = both.transpose(3, 2, 0, 1, 4).reshape(KO, P, CHUNK)
    return chunks


def expert_params(a):
    par = np.zeros((P, EXP_COLS), np.float32)
    par[:, E_KEYS:E_KEYS + NKEYS] = a["peer_keys_1"][0].T
    par[:, E_KEYS + NKEYS:E_IDENT] = a["peer_keys_2"][0].T
    par[:, E_IDENT:E_FFNW] = np.eye(P)
    par[:, E_FFNW:E_FINW] = a["ffn_norm_w"][0]
    par[:, E_FINW:E_IOTA] = a["final_norm_w"]
    par[:, E_IOTA:] = np.arange(TOPK)
    return par


def kernel(**inputs):
    import concourse.bacc as _bacc
    from concourse.bass_utils import run_bass_kernel_spmd as _run

    a = {k: np.asarray(v) for k, v in inputs.items()}
    arrays = {
        "x": a["x"][0].reshape(TILES, P, D),
        "weights": mixer_weights(a),
        "mix_params": mixer_params(a),
        "experts": np.ascontiguousarray(np.concatenate([a["peer_u"][0], a["peer_v"][0]], axis=1)),
        "w_out": np.ascontiguousarray(a["w_out"][0].reshape(KO, P, D).transpose(1, 0, 2)),
        "w_query": np.ascontiguousarray(a["peer_w_q"][0].reshape(KO, P, PH, 2 * NKEYS).transpose(1, 2, 0, 3)),
        "exp_params": expert_params(a),
    }
    nc = _bacc.Bacc("TRN2", target_bir_lowering=False, num_devices=1)
    d = {n: nc.dram_tensor(f"in_{n}", v.shape, F32, kind="ExternalInput").ap() for n, v in arrays.items()}
    merged = nc.dram_tensor("merged_branches", (TILES, P, D), F32, kind="Internal").ap()
    out = nc.dram_tensor("out", (1, SEQ, D), F32, kind="ExternalOutput").ap()
    mixer_block(nc, d["x"], d["weights"], d["mix_params"], merged)
    expert_block(nc, d["x"], merged, d["w_out"], d["experts"], d["w_query"], d["exp_params"],
                 out[0].rearrange("(t p) d -> t p d", p=P))
    r = _run(nc, [{f"in_{n}": v for n, v in arrays.items()}], core_ids=[0])
    return r.results[0]["out"]
```

```python
from contextlib import ExitStack

import numpy as np

import concourse.bass as bass
from concourse import mybir

ALU = mybir.AluOpType
ACT = mybir.ActivationFunctionType
AX = mybir.AxisListType
F32 = mybir.dt.float32
F32R = mybir.dt.float32r
U32 = mybir.dt.uint32

P = 128
D = 1024
SEQ = 1024
TILES = SEQ // P
KO = D // P
HEADS = 8
KV_HEADS = 2
HD = 64
WIDTH = HEADS * HD
WB = WIDTH // P
BUCKETS = 32
MAX_DISTANCE = 128
EPS = 1e-6
NEG_INF = -1e30

GROUP = 512
GROUPS = SEQ // GROUP
GT = GROUP // P
ALIGN = 32
BANKS = 4

SLOTS = 8
CHUNK = D
STAGES = 4
SPLITS = 2
QKV_CHUNKS = WB + 2
ROUNDS = 5

N_Q = 0
N_K = N_Q + WB
N_V = N_K + 1
N_GU = N_V + 1
N_GV = N_GU + WB
N_GATE = N_GV + GT
N_BRANCH = N_GATE + 2 * KO
N_ALL = N_BRANCH + 2 * KO
GATES_PER_TILE = 2 * KO // GT
TURN_FROM = 2
FIRST_FROM = 3
CHUNKS = ROUNDS * SLOTS - (SLOTS - QKV_CHUNKS)

PH = 8
NKEYS = 128
TOPK = 16
RING = 8
BATCH = 2
BATCHES = TOPK // BATCH
FINISH_AT = 3
LOWEST = -3.0e38

C_IDENT = 0
C_MIXW = C_IDENT + P
C_SINK = C_MIXW + D
C_LNW = C_SINK + HEADS
C_LNB = C_LNW + WIDTH
C_BS = C_LNB + WIDTH
C_WS = C_BS + WB * P
C_OWN01 = C_WS + HEADS * P
C_PREV01 = C_OWN01 + P
C_OWNNEG = C_PREV01 + P
C_PREVNEG = C_OWNNEG + P
MIX_COLS = C_PREVNEG + P
R_DIST = 0
R_REL = R_DIST + 2 * P
R_FLIP = R_REL + HEADS
REL_COLS = R_FLIP + P
E_KEYS = 0
E_IDENT = E_KEYS + 2 * NKEYS
E_FFNW = E_IDENT + P
E_FINW = E_FFNW + D
E_IOTA = E_FINW + D
EXP_COLS = E_IOTA + TOPK


class Chain:

    def __init__(self, eng, sem):
        self.eng, self.sem, self.n = eng, sem, 0

    def mark(self, ins):
        self.n += 1
        return ins.then_inc(self.sem, 1)

    def wait(self):
        self.eng.wait_ge(self.sem, self.n)

    def step(self, ins):
        self.mark(ins)
        self.wait()

    def restart(self):
        self.eng.sem_clear(self.sem)
        self.n = 0


class Names:
    pass


def shared_memory(nc, ctx):
    m = Names()

    def sb(name, shape, dt=F32):
        return ctx.enter_context(nc.sbuf_tensor(name, shape, dt))

    def sem(name):
        return ctx.enter_context(nc.semaphore(name))

    def base():
        return -(-nc.sbuf_base // ALIGN) * ALIGN

    def over(name, shape, at):
        return nc.alloc_sbuf_tensor_at(name, shape, F32R, offset=at)[:]

    at = base()
    m.wout = sb("wout", [P, KO, D])
    m.hT_high = over("hT_high", [P, KO, GROUP], at)
    m.hT_low = over("hT_low", [P, KO, GROUP], at + 4 * KO * GROUP)
    m.wq = sb("wq", [P, PH, KO, 2 * NKEYS])
    by_head = m.wq[:].rearrange("p h k m -> p h (k m)")
    m.x = by_head[:, 0:2, :].rearrange("p h c -> p (h c)").rearrange("p (t d) -> p t d", t=GT)
    m.qT = by_head[:, 2, :].rearrange("p (b t) -> p b t", b=WB)
    m.bias_own = by_head[:, 3, 0:HEADS * P].rearrange("p (h j) -> p h j", h=HEADS)
    m.bias_prev = by_head[:, 3, HEADS * P:].rearrange("p (h j) -> p h j", h=HEADS)
    m.stage = by_head[:, 4:6, :].rearrange("p h c -> p (h c)").rearrange("p (s c) -> p s c", s=STAGES)
    m.guv = by_head[:, 6:PH, :].rearrange("p h c -> p (h c)")
    at = base()
    m.rows = sb("rows", [P, RING, 2 * D])
    m.gates = m.rows[:, 0:4, :].rearrange("p s c -> p (s c)").rearrange("p (n t) -> p n t", n=2 * KO)
    m.attnT_high, m.attnT_low, m.gmlpT_high, m.gmlpT_low = [
        over(name, [P, WB, GROUP], at + 4 * s * 2 * D)
        for s, name in ((4, "attnT_high"), (5, "attnT_low"), (6, "gmlpT_high"), (7, "gmlpT_low"))]
    tile_in = sb("tile_in", [P, 2 * HEADS * P + HEADS])
    m.probs = tile_in[:, 0:HEADS * P + HEADS]
    m.pt_own = tile_in[:, HEADS * P + HEADS:].rearrange("p (h i) -> p h i", h=HEADS)
    m.xt = tile_in[:, 0:D]
    m.mt = tile_in[:, HEADS * P + HEADS:].rearrange("p (k m) -> p k m", k=KO)
    params = sb("params", [P, MIX_COLS])
    m.mix_par = params[:, 0:MIX_COLS]
    m.par = params[:, 0:EXP_COLS]
    m.h2T = params[:, EXP_COLS:EXP_COLS + D].rearrange("p (k m) -> p k m", k=KO)
    m.qtok = params[:, EXP_COLS + D:EXP_COLS + D + 2 * P]
    m.qhT = params[:, EXP_COLS + D + 2 * P:EXP_COLS + D + 4 * P].rearrange("p (c m) -> p c m", c=2)
    kv = sb("kv", [P, P + GROUP + (GT + 1) * P])
    m.kT = kv[:, 0:P + GROUP]
    m.vtok = kv[:, P + GROUP:].rearrange("p (t m) -> p t m", t=GT + 1)
    m.hnext = kv[:, 0:D]
    m.val = sb("val", [P, 2, TOPK])
    m.ind = sb("ind", [P, 2, TOPK], U32)
    m.best = sb("best", [P, TOPK])
    m.pos = sb("pos", [P, TOPK], U32)
    m.digits = sb("digits", [P, 2, TOPK], U32)
    m.picked = sb("picked", [P, 2, TOPK])
    m.index = sb("index", [P, 2, TOPK], U32)
    m.negtop = sb("negtop", [P, 1])
    m.expo = sb("expo", [P, TOPK])
    m.esum = sb("esum", [P, 1])
    m.resum = sb("resum", [P, 1])
    m.gate = sb("gate", [P, 2, TOPK])
    m.ss = sb("ess", [P, 1])
    m.rms = sb("erms", [P, 1])
    m.rstd = sb("erstd", [P, 1])
    m.eps = sb("eps", [P, 1])

    banks = ctx.enter_context(nc.psum_tensor("banks", [P, 2 * BANKS, GROUP], F32))
    m.bank = banks[:, 0:BANKS, :]
    m.lflat = banks[:, BANKS:, :].rearrange("p b c -> p (b c)")
    m.y = banks[:, 0:2, :]
    m.mixed = banks[:, BANKS:BANKS + 2, :]
    m.turned = banks[:, BANKS + 2:, :].rearrange("p b c -> p (b c)").rearrange("p (k m) -> p k m", k=KO)

    def work(first_bank, buffer):
        w = Names()
        w.query = banks[:, first_bank, :]
        w.match = banks[:, first_bank + 1, 0:2 * NKEYS].rearrange("p (c k) -> p c k", c=2)
        w.scores = buffer[:, 0:2 * NKEYS].rearrange("p (c k) -> p c k", c=2)
        w.rest = buffer[:, 2 * NKEYS:4 * NKEYS].rearrange("p (c k) -> p c k", c=2)
        w.cand = buffer[:, 4 * NKEYS:4 * NKEYS + TOPK * TOPK]
        w.cand_rest = buffer[:, 4 * NKEYS + TOPK * TOPK:4 * NKEYS + 2 * TOPK * TOPK]
        w.onehot = buffer[:, 4 * NKEYS:4 * NKEYS + 2 * TOPK * TOPK].rearrange("p (c k m) -> p c k m", c=2, k=TOPK)
        return w

    m.first_work = work(BANKS, m.gates[:, 0:2, :].rearrange("p a b -> p (a b)"))
    m.work_in = lambda buffer: work(2, buffer)

    m.merged_stored = sem("merged_stored")
    m.expert_params_in = sem("expert_params_in")
    m.wout_in = [sem(f"wout_in{c}") for c in range(2)]
    m.wq_first_in = sem("wq_first_in")
    m.wq_middle_in = sem("wq_middle_in")
    m.wq_late_in = sem("wq_late_in")
    m.wq_last_in = sem("wq_last_in")
    m.mt_loaded = sem("mt_loaded")
    m.xt_loaded = sem("xt_loaded")
    m.mixed_done = sem("mixed_done")
    m.x2_ready = sem("x2_ready")
    m.rms_ready = sem("tile_rms_ready")
    m.hnext_ready = sem("hnext_ready")
    m.turned_done = sem("turned_done")
    m.h2T_ready = sem("h2T_ready")
    m.query_done = sem("query_done")
    m.query_out = sem("query_out")
    m.qturn_done = sem("qturn_done")
    m.qhT_ready = sem("qhT_ready")
    m.match_done = sem("match_done")
    m.scores_ready = sem("scores_ready")
    m.scores_seen = sem("scores_seen")
    m.scores_free = sem("scores_free")
    m.best_ready = sem("best_ready")
    m.expo_ready = sem("expo_ready")
    m.index_ready = sem("index_ready")
    return m


def expert_tensor(pe, mem, work):
    ident = mem.par[:, E_IDENT:E_IDENT + P]

    def mix(t, halves=range(2), before=None):
        pe.wait_ge(mem.mt_loaded, 16 * t + 16)
        for c in halves:
            pe.wait_ge(mem.wout_in[c], 16)
            for k in range(KO):
                last = pe.matmul(mem.mixed[:, c, :], mem.mt[:, k, :], mem.wout[:, k, c * GROUP:(c + 1) * GROUP],
                                 start=(k == 0), stop=(k == KO - 1))
                if before is not None and c == 0 and k == 0:
                    before(last)
        if 1 in halves:
            last.then_inc(mem.mixed_done, 1)

    def turn(t):
        pe.wait_ge(mem.hnext_ready, t + 1)
        for k in range(KO):
            last = pe.transpose(mem.turned[:, k, :], mem.hnext[:, k * P:(k + 1) * P], ident)
        last.then_inc(mem.turned_done, 1)

    def ask(i, h):
        for k in range(KO):
            w = mem.wq[:, bass.ds(h, 1), k, :].rearrange("p h m -> p (h m)")
            last = pe.matmul(work.query[:, 0:2 * P], mem.h2T[:, k, :], w, start=(k == 0), stop=(k == KO - 1))
        last.then_inc(mem.query_done, 1)

    def turn_query(i):
        pe.wait_ge(mem.query_out, i + 1)
        for half in range(2):
            last = pe.transpose(work.query[:, (2 + half) * P:(3 + half) * P], mem.qtok[:, half * P:(half + 1) * P], ident)
        last.then_inc(mem.qturn_done, 1)

    def match_keys(i):
        pe.wait_ge(mem.qhT_ready, i + 1)
        for half in range(2):
            keys = mem.par[:, E_KEYS + half * NKEYS:E_KEYS + (half + 1) * NKEYS]
            last = pe.matmul(work.match[:, half, :], mem.qhT[:, half, :], keys, start=True, stop=True)
        last.then_inc(mem.match_done, 1)

    steps = Names()
    steps.mix, steps.turn, steps.ask, steps.turn_query, steps.match_keys = mix, turn, ask, turn_query, match_keys
    return steps


def expert_scalar(act, mem, work, chain):
    squares = mem.turned.rearrange("p k m -> p (k m)")

    def norm_in(t):
        act.wait_ge(mem.x2_ready, t + 1)
        chain.step(act.activation(squares, mem.xt, ACT.Square, accum_out=mem.ss[:]))
        act.activation(mem.rms[:], mem.ss[:], ACT.Sqrt, bias=mem.eps[:, 0:1], scale=1.0 / D).then_inc(mem.rms_ready, 1)

    def take_turned(t):
        act.wait_ge(mem.turned_done, t + 1)
        act.activation(mem.h2T, mem.turned, ACT.Copy).then_inc(mem.h2T_ready, 1)

    def take_query(i):
        act.wait_ge(mem.query_done, i + 1)
        act.activation(mem.qtok, work.query[:, 0:2 * P], ACT.Copy).then_inc(mem.query_out, 1)

    def take_turned_query(i):
        act.wait_ge(mem.qturn_done, i + 1)
        act.activation(mem.qhT.rearrange("p h m -> p (h m)"), work.query[:, 2 * P:4 * P], ACT.Copy).then_inc(mem.qhT_ready, 1)

    def take_scores(i):
        act.wait_ge(mem.match_done, i + 1)
        act.wait_ge(mem.scores_free, i + 1)
        act.activation(work.scores, work.match, ACT.Copy).then_inc(mem.scores_ready, 1)

    def numerators(i):
        act.wait_ge(mem.best_ready, i + 1)
        act.activation(mem.expo[:], mem.best[:], ACT.Exp, bias=mem.negtop[:, 0:1], accum_out=mem.esum[:]).then_inc(mem.expo_ready, 1)

    steps = Names()
    steps.norm_in, steps.take_turned, steps.take_query = norm_in, take_turned, take_query
    steps.take_turned_query, steps.take_scores, steps.numerators = take_turned_query, take_scores, numerators
    return steps


def expert_vector(dve, mem, work, chain):
    mark, step = chain.mark, chain.step
    iota = mem.par[:, E_IOTA:E_IOTA + TOPK]

    def residual(t):
        dve.wait_ge(mem.xt_loaded, 16 * t + 16)
        dve.wait_ge(mem.mixed_done, t + 1)
        dve.tensor_tensor(mem.xt, mem.xt, mem.mixed.rearrange("p c m -> p (c m)"), ALU.add).then_inc(mem.x2_ready, 1)

    def norm_in(t):
        dve.wait_ge(mem.rms_ready, t + 1)
        step(dve.reciprocal(mem.rstd[:], mem.rms[:]))
        step(dve.scalar_tensor_tensor(out=mem.hnext, in0=mem.xt, scalar=mem.rstd[:, 0:1], in1=mem.par[:, E_FFNW:E_FFNW + D],
                                      op0=ALU.mult, op1=ALU.mult))
        dve.sem_inc(mem.hnext_ready, 1)

    def top(values, spare_values, found, places, sets):
        for c in range(sets):
            mark(dve.max(found[c][:, 0:8], values[c]))
        chain.wait()
        for c in range(sets):
            mark(dve.max_index(places[c][:, 0:8], found[c][:, 0:8], values[c]))
            mark(dve.match_replace(spare_values[c], found[c][:, 0:8], values[c], LOWEST))
        chain.wait()
        for c in range(sets):
            mark(dve.max(found[c][:, 8:16], spare_values[c]))
        chain.wait()
        for c in range(sets):
            mark(dve.max_index(places[c][:, 8:16], found[c][:, 8:16], spare_values[c]))
        chain.wait()

    def best_of_sets(i):
        dve.wait_ge(mem.scores_ready, i + 1)
        dve.sem_inc(mem.scores_seen, 1)
        top([work.scores[:, c, :] for c in range(2)], [work.rest[:, c, :] for c in range(2)],
            [mem.val[:, c, :] for c in range(2)], [mem.ind[:, c, :] for c in range(2)], 2)
        dve.sem_inc(mem.scores_free, 1)

    def best_of_sums():
        sums = work.cand.rearrange("p (a b) -> p a b", a=TOPK)
        step(dve.tensor_tensor(sums, mem.val[:, 0, :].unsqueeze(2).to_broadcast([P, TOPK, TOPK]),
                               mem.val[:, 1, :].unsqueeze(1).to_broadcast([P, TOPK, TOPK]), ALU.add))
        top([work.cand], [work.cand_rest],
            [mem.best[:]], [mem.pos[:]], 1)
        step(dve.tensor_scalar(mem.negtop[:], mem.best[:, 0:1], -1.0, None, ALU.mult))
        dve.sem_inc(mem.best_ready, 1)

    def indices(j):
        mark(dve.tensor_scalar(mem.digits[:, 0, :], mem.pos[:], 4, None, ALU.logical_shift_right))
        step(dve.tensor_scalar(mem.digits[:, 1, :], mem.pos[:], TOPK - 1, None, ALU.bitwise_and))
        step(dve.tensor_tensor(work.onehot.rearrange("p c k m -> p (c k) m"),
                               mem.digits[:].rearrange("p c k -> p (c k)").unsqueeze(2).to_broadcast([P, 2 * TOPK, TOPK]),
                               iota.unsqueeze(1).to_broadcast([P, 2 * TOPK, TOPK]), ALU.is_equal))
        step(dve.tensor_tensor(work.onehot, work.onehot, mem.ind[:].unsqueeze(2).to_broadcast([P, 2, TOPK, TOPK]), ALU.mult))
        step(dve.tensor_reduce(mem.picked[:].rearrange("p c k -> p (c k)"), work.onehot.rearrange("p c k m -> p (c k) m"),
                               AX.X, ALU.add))
        dve.scalar_tensor_tensor(out=mem.index[:, j, :], in0=mem.picked[:, 0, :], scalar=float(NKEYS), in1=mem.picked[:, 1, :],
                                 op0=ALU.mult, op1=ALU.add).then_inc(mem.index_ready, 1)

    def normalise(i, j):
        dve.wait_ge(mem.expo_ready, i + 1)
        step(dve.reciprocal(mem.resum[:], mem.esum[:]))
        step(dve.tensor_scalar(mem.gate[:, j, :], mem.expo[:], mem.resum[:, 0:1], None, ALU.mult))

    steps = Names()
    steps.residual, steps.norm_in, steps.best_of_sets = residual, norm_in, best_of_sets
    steps.best_of_sums, steps.indices, steps.normalise = best_of_sums, indices, normalise
    return steps


def mixer_block(nc, mem, x_in, weights, mix_params, rel_params, rel_table, w_out, w_query, exp_params, merged_out):
    with ExitStack() as ctx:
        def sb(name, shape, dt=F32):
            return ctx.enter_context(nc.sbuf_tensor(name, shape, dt))

        def sem(name):
            return ctx.enter_context(nc.semaphore(name))

        x = mem.x
        hT_high, hT_low = mem.hT_high, mem.hT_low
        qT = mem.qT
        kT = mem.kT
        vtok = mem.vtok
        guv = mem.guv
        guT = guv[:, 0:WB * GROUP].rearrange("p (b t) -> p b t", b=WB)
        gv = guv[:, WB * GROUP:].rearrange("p (t m) -> p t m", t=GT)
        merged = guv.rearrange("p (t k m) -> p t k m", t=GT, k=KO)
        gates = mem.gates
        attnT_high, attnT_low, gmlpT_high, gmlpT_low = mem.attnT_high, mem.attnT_low, mem.gmlpT_high, mem.gmlpT_low
        stage = mem.stage
        w_high = sb("w_high", [P, SPLITS, CHUNK], F32R)
        w_low = sb("w_low", [P, SPLITS, CHUNK], F32R)
        par = mem.mix_par
        bias_own, bias_prev = mem.bias_own, mem.bias_prev
        before_first = sb("before_first", [P, 1])
        probs = mem.probs
        pt_own = mem.pt_own
        pt_prev = probs[:, 0:HEADS * P].rearrange("p (h i) -> p h i", h=HEADS)
        ss = sb("ss", [P, GT])
        rms = sb("rms", [P, GT])
        rstd = sb("rstd", [P, GT])
        top = sb("top", [P, HEADS])
        den = sb("den", [P, HEADS])
        rden = sb("rden", [P, HEADS])
        stats = sb("stats", [P, GT, 6])
        mv = sb("mv", [P, GT, 2])
        ln_std = sb("ln_std", [P, GT])
        ln_rstd = sb("ln_rstd", [P, GT])
        eps = mem.eps

        bank = mem.bank
        lflat = mem.lflat
        logits = lflat.rearrange("p (h j) -> p h j", h=HEADS)
        ptT = lflat[:, 0:HEADS * P].rearrange("p (h i) -> p h i", h=HEADS)
        pv = lflat[:, HEADS * P:HEADS * P + WB * P].rearrange("p (b i) -> p b i", b=WB)
        sg = lflat[:, HEADS * P + WB * P:HEADS * P + 2 * WB * P].rearrange("p (b i) -> p b i", b=WB)

        ident = par[:, C_IDENT:C_IDENT + P]
        turned = lflat[:, 0:D].rearrange("p (k m) -> p k m", k=KO)
        rel_par = gates[:, 0, :][:, 0:REL_COLS]
        by_distance = gates[0:HEADS, 1, :][:, 0:2 * P]
        hankel = gates[:, 2:4, :].rearrange("p a b -> p (a b)").rearrange("p (h j) -> p h j", h=HEADS)
        rel = lflat[:, 0:HEADS * P]

        params_in = sem("params_in")
        late_params_in = sem("late_params_in")
        rel_params_in = sem("rel_params_in")
        table_done = sem("table_done")
        table_out = sem("table_out")
        table_stored = sem("table_stored")
        hankel_in = sem("hankel_in")
        turned_done = sem("x_turned")
        hT_high_ready = sem("hT_high_ready")
        x_loaded = [sem(f"x_loaded{t}") for t in range(GT)]
        x_claimed = sem("x_claimed")
        stage_loaded = [sem(f"stage_loaded{s}") for s in range(STAGES)]
        high_ready = sem("high_ready")
        split_ready = sem("split_ready")
        split_free = sem("split_free")
        hT_ready = sem("hT_ready")
        consts_set = sem("consts_set")
        rms_ready = sem("rms_ready")
        hn_ready = sem("hn_ready")
        product_done = sem("product_done")
        act_taken = sem("act_taken")
        dve_taken = sem("dve_taken")
        rel_done = sem("rel_done")
        bias_ready = sem("bias_ready")
        carry_ready = sem("carry_ready")
        ln_var = sem("ln_var")
        ln_std_ready = sem("ln_std_ready")
        vln_ready = sem("vln_ready")
        logits_done = sem("logits_done")
        shifted_ready = sem("shifted_ready")
        exp_done = sem("exp_done")
        probs_ready = sem("probs_ready")
        pt_done = sem("pt_done")
        pt_masked = sem("pt_masked")
        pv_done = sem("pv_done")
        sg_done = sem("sg_done")
        branch_in = sem("branch_in")
        merged_ready = sem("merged_ready")
        merged_stored = mem.merged_stored
        store_claimed = sem("store_claimed")
        dve_chain = sem("dve_chain")
        act_chain = sem("act_chain")

        block = ctx.enter_context(nc.Block())

        def run_groups(eng, group):
            with eng.Fori(0, GROUPS - 1) as g:
                group(g, False)
            group(GROUPS - 1, True)

        def chunk_number(r, s):
            return r * SLOTS + s - (0 if isinstance(r, int) and r == 0 else SLOTS - QKV_CHUNKS)

        def stage_loads(g, r, s):
            nth = s // STAGES
            if s % STAGES < QKV_CHUNKS - STAGES:
                return g * (2 * ROUNDS) + (r * 2 + nth)
            return g * (2 * ROUNDS - 1) + (r * 2 + nth - (1 if r > 0 else 0))

        @block.sync
        def _(sp):
            def stage_free(g, n):
                sp.wait_ge(split_ready, g * CHUNKS + (n + 1))

            def group(g, last):
                for s in range(STAGES, QKV_CHUNKS):
                    stage_free(g, s)
                    sp.dma_start(stage[:, s % STAGES, :], weights[s]).then_inc(stage_loaded[s % STAGES], 16)
                for s in range(SLOTS):
                    stage_free(g, chunk_number(1, s) + (SLOTS - QKV_CHUNKS if s < QKV_CHUNKS - STAGES else 0))
                    sp.dma_start(stage[:, s % STAGES, :], weights[SLOTS + s]).then_inc(stage_loaded[s % STAGES], 16)
                sp.wait_ge(hT_ready, g * (2 * GT) + 2 * GT)
                sp.sem_inc(x_claimed, 1)
                if last:
                    sp.dma_start(mem.wq[:, 0:2], w_query[:, 0:2]).then_inc(mem.wq_first_in, 16)
                else:
                    for t in range(GT):
                        sp.dma_start(x[:, t, :], x_in[bass.ds((g + 1) * GT + t, 1)].rearrange(
                            "t p d -> (t p) d")).then_inc(x_loaded[t], 16)
                with sp.Fori(2, ROUNDS - 1) as r:
                    for s in range(SLOTS):
                        chunk = sp.snap(r * SLOTS + s)
                        stage_free(g, chunk_number(r, s))
                        sp.dma_start(stage[:, s % STAGES, :], weights[bass.ds(chunk, 1)].rearrange(
                            "c p d -> (c p) d")).then_inc(stage_loaded[s % STAGES], 16)
                for s in range(SLOTS):
                    stage_free(g, chunk_number(ROUNDS - 1, s))
                    sp.dma_start(stage[:, s % STAGES, :], weights[(ROUNDS - 1) * SLOTS + s]).then_inc(
                        stage_loaded[s % STAGES], 16)
                    if last and s == STAGES - 1:
                        sp.wait_ge(branch_in, GROUPS * (2 * GT))
                        sp.wait_ge(merged_stored, 32 * GROUPS)
                        sp.dma_start(mem.mt.rearrange("p k m -> p (k m)"), merged_out[0]).then_inc(mem.mt_loaded, 16)
                        sp.dma_start(mem.xt, x_in[0]).then_inc(mem.xt_loaded, 16)
                        sp.wait_ge(act_taken, GROUPS * N_BRANCH)
                    if last and STAGES <= s < STAGES + 2:
                        cols = slice((s - STAGES) * GROUP, (s - STAGES + 1) * GROUP)
                        sp.dma_start(mem.wout[:, :, cols], w_out[:, :, cols]).then_inc(mem.wout_in[s - STAGES], 16)
                    if last and s == STAGES + 2:
                        sp.dma_start(mem.par, exp_params).then_inc(mem.expert_params_in, 16)
                if last:
                    sp.dma_start(mem.wq[:, 2:4], w_query[:, 2:4]).then_inc(mem.wq_middle_in, 16)
                    sp.wait_ge(split_ready, STAGES + GROUPS * CHUNKS)
                    sp.dma_start(mem.wq[:, 4:6], w_query[:, 4:6]).then_inc(mem.wq_late_in, 16)
                else:
                    for s in range(STAGES):
                        stage_free(g + 1, s)
                        sp.dma_start(stage[:, s, :], weights[s]).then_inc(stage_loaded[s], 16)
                first_tile = g * GT if last else sp.snap(g * GT)
                for half in range(2):
                    cols = slice(half * D // 2, (half + 1) * D // 2)
                    sp.wait_ge(merged_ready, g * KO + (half + 1) * KO // 2)
                    sp.sem_inc(store_claimed, 1)
                    sp.dma_start(merged_out[bass.ds(first_tile, GT), :, cols].rearrange("t p d -> p t d"),
                                 guv.rearrange("p (t d) -> p t d", t=GT)[:, :, cols]).then_inc(merged_stored, 16)

            def load_x(t):
                sp.dma_start(x[:, t, :], x_in[t]).then_inc(x_loaded[t], 16)

            def load_first(s):
                sp.dma_start(stage[:, s, :], weights[s]).then_inc(stage_loaded[s], 16)

            sp.sem_inc(merged_stored, 32)
            sp.dma_start(rel_par, rel_params).then_inc(rel_params_in, 16)
            load_x(0)
            sp.dma_start(par[:, 0:C_SINK], mix_params[:, 0:C_SINK]).then_inc(params_in, 16)
            load_x(1)
            sp.wait_ge(table_out, 1)
            sp.dma_start(rel_table, by_distance).then_inc(table_stored, 16)
            load_x(2)
            load_x(3)
            load_first(0)
            sp.wait_ge(table_stored, 16)
            sp.dma_start(hankel, bass.AP(rel_table.tensor, 0, [[1, P], [2 * P, HEADS], [1, P]])).then_inc(hankel_in, 16)
            for s in range(1, STAGES):
                load_first(s)
            sp.dma_start(par[:, C_SINK:], mix_params[:, C_SINK:]).then_inc(late_params_in, 16)
            run_groups(sp, group)

        @block.gpsimd
        def _(pool):
            pool.sem_inc(split_ready, STAGES)

            def group(g, last):
                for r in range(ROUNDS):
                    for s in range(QKV_CHUNKS if r == 0 else SLOTS):
                        n = chunk_number(r, s)
                        pool.wait_ge(high_ready, g * CHUNKS + (n + 1))
                        pool.tensor_tensor(w_low[:, n % SPLITS, :], stage[:, s % STAGES, :],
                                           w_high[:, n % SPLITS, :].bitcast(F32), ALU.subtract).then_inc(split_ready, 1)

            run_groups(pool, group)

        @block.tensor
        def _(pe):
            experts = expert_tensor(pe, mem, mem.first_work)
            pe.sem_inc(split_free, SPLITS)
            pe.wait_ge(rel_params_in, 16)
            pe.matmul(bank[0:HEADS, BANKS - 1, 0:2 * P], rel_par[0:BUCKETS, R_REL:R_REL + HEADS],
                      rel_par[0:BUCKETS, R_DIST:R_DIST + 2 * P], start=True, stop=True).then_inc(table_done, 1)

            def turn(g, t):
                pe.wait_ge(hn_ready, g * GT + (t + 1))
                for half in range(2):
                    if t > 0:
                        pe.wait_ge(hT_ready, g * (2 * GT) + 2 * t - 1 + half)
                    for k in range(half * WB, (half + 1) * WB):
                        last = pe.transpose(turned[:, k, :], x[:, t, k * P:(k + 1) * P], ident)
                    last.then_inc(turned_done, 1)

            pe.wait_ge(params_in, 16)
            for t in range(GT):
                turn(0, t)
            pe.wait_ge(table_out, 1)
            pe.wait_ge(hankel_in, 16)
            for c in range(2):
                pe.wait_ge(hT_ready, 2 * GT - 1 + c)
                last = pe.matmul(rel[:, c * GROUP:(c + 1) * GROUP], rel_par[:, R_FLIP:R_FLIP + P],
                                 hankel[:, c * WB:(c + 1) * WB, :], start=True, stop=True)
            last.then_inc(rel_done, 1)

            def group(g, final):
                def bank_free(n):
                    if n < BANKS:
                        before = N_ALL - 1 - (N_ALL - 1 - n) % BANKS
                        pe.wait_ge(dve_taken, g * (N_ALL - N_BRANCH) + (before - N_ALL + 1 + BANKS))
                    elif n - BANKS >= N_BRANCH:
                        pe.wait_ge(dve_taken, g * (N_ALL - N_BRANCH) + (n - N_BRANCH + 1))
                    else:
                        pe.wait_ge(act_taken, g * N_BRANCH + (n - BANKS + 1))

                def chunk_in(r, s, shape, **dims):
                    n = chunk_number(r, s)
                    pe.wait_ge(split_ready, g * CHUNKS + (n + 1 + STAGES))
                    return [w[:, n % SPLITS, :].rearrange(shape, **dims) for w in (w_high, w_low)]

                used = []

                def release(ins):
                    if used:
                        used.pop()
                        ins.then_inc(split_free, 1)

                def three(out, stationary, moving, start, stop):
                    first = pe.matmul(out, stationary[0], moving[0], start=start, stop=False)
                    pe.matmul(out, stationary[0], moving[1], start=False, stop=False)
                    return first, pe.matmul(out, stationary[1], moving[0], start=False, stop=stop)

                def rows_of_weights(n, r, s):
                    w = chunk_in(r, s, "p (k m) -> p k m", k=KO)
                    bank_free(n)
                    for k in range(KO):
                        first, last = three(bank[:, n % BANKS, :], [a[:, k, :] for a in w],
                                            [hT_high[:, k, :], hT_low[:, k, :]], k == 0, k == KO - 1)
                        if k == 0:
                            release(first)
                    last.then_inc(product_done, 1)
                    used.append(n)

                pe.wait_ge(hT_ready, g * (2 * GT) + 2 * GT)
                for b in range(WB + 1):
                    rows_of_weights(N_Q + b, 0, b)

                def tokens(k, t):
                    return [a[:, k, t * P:(t + 1) * P] for a in (hT_high, hT_low)]

                w = chunk_in(0, WB + 1, "p (k m) -> p k m", k=KO)
                bank_free(N_V)
                for t in range(GT):
                    for k in range(KO):
                        first, last = three(bank[:, N_V % BANKS, t * P:(t + 1) * P], tokens(k, t), [a[:, k, :] for a in w],
                                            k == 0, k == KO - 1)
                        if t == 0 and k == 0:
                            release(first)
                last.then_inc(product_done, 1)
                used.append(N_V)
                for b in range(WB):
                    rows_of_weights(N_GU + b, 1, b)
                for c in range(4):
                    w = chunk_in(1, WB + c, "p (k m) -> p k m", k=2)
                    for t in range(GT):
                        if c == 0:
                            bank_free(N_GV + t)
                        for k in range(2):
                            first, last = three(bank[:, (N_GV + t) % BANKS, :], tokens(2 * c + k, t), [a[:, k, :] for a in w],
                                                c == 0 and k == 0, c == 3 and k == 1)
                            if t == 0 and k == 0:
                                release(first)
                        if c == 3:
                            last.then_inc(product_done, 1)
                    used.append(N_GV + c)

                for t in range(GT):
                    gate_products = range(GATES_PER_TILE * t, GATES_PER_TILE * (t + 1))

                    def gate(c):
                        c = gate_products[c]
                        rows_of_weights(N_GATE + c, 2 + c // SLOTS, c % SLOTS)

                    pe.wait_ge(act_taken, g * N_BRANCH + (N_V + 1))
                    pe.wait_ge(bias_ready, 1)
                    if t > 0:
                        pe.wait_ge(branch_in, g * 2 * GT + 2 * t)
                    for h in range(HEADS):
                        kv, b = h // WB, h % WB
                        rows = slice(kv * HD, (kv + 1) * HD)
                        last = pe.matmul(logits[:, h, :], qT[rows, b, t * P:(t + 1) * P], kT[rows, t * P:(t + 2) * P],
                                         start=True, stop=True)
                        if h == 0:
                            release(last)
                    last.then_inc(logits_done, 1)
                    gate(0)
                    gate(1)
                    pe.wait_ge(shifted_ready, g * GT + t + 1)
                    pe.wait_ge(vln_ready, g * GT + t + 1)
                    for q in range(HEADS):
                        last = pe.matmul(sg[(q % 2) * HD:(q % 2 + 1) * HD, q // 2, :], gv[:, t, q * HD:(q + 1) * HD],
                                         par[:, C_WS + q * P:C_WS + (q + 1) * P], start=True, stop=True)
                        if q == 0:
                            release(last)
                    last.then_inc(sg_done, 1)
                    pe.wait_ge(probs_ready, g * GT + t + 1)
                    for h in range(HEADS):
                        last = pe.transpose(ptT[:, h, :], probs[:, h * P:(h + 1) * P], ident)
                    last.then_inc(pt_done, 1)
                    gate(2)
                    pe.wait_ge(pt_masked, g * GT + t + 1)
                    for h in range(HEADS):
                        kv, b = h // WB, h % WB
                        cols = slice(kv * HD, (kv + 1) * HD)
                        first = pe.matmul(pv[cols, b, :], vtok[:, t, cols], pt_prev[:, h, :], start=True, stop=False)
                        if h == 0:
                            release(first)
                        last = pe.matmul(pv[cols, b, :], vtok[:, t + 1, cols], pt_own[:, h, :], start=False, stop=True)
                    last.then_inc(pv_done, 1)
                    gate(3)

                pe.wait_ge(branch_in, g * 2 * GT + 2 * GT)
                for m in range(KO):
                    w = chunk_in(4, m, "p (b k m) -> p b k m", b=2, k=WB)
                    for br, src in enumerate(((attnT_high, attnT_low), (gmlpT_high, gmlpT_low))):
                        if final and m == FIRST_FROM + 3 and br == 1:
                            experts.turn_query(0)
                        n = N_BRANCH + 2 * m + br
                        bank_free(n)
                        for k in range(WB):
                            first, last = three(bank[:, n % BANKS, :], [a[:, br, k, :] for a in w], [a[:, k, :] for a in src],
                                                k == 0, k == WB - 1)
                            if br == 0 and k == 0:
                                release(first)
                        last.then_inc(product_done, 1)
                    used.append(m)
                    if not final and TURN_FROM <= m < TURN_FROM + GT:
                        turn(g + 1, m - TURN_FROM)
                    if final and m == FIRST_FROM:
                        experts.mix(0, before=release)
                    if final and m == FIRST_FROM + 1:
                        pe.wait_ge(mem.expert_params_in, 16)
                        experts.turn(0)
                    if final and m == FIRST_FROM + 2:
                        pe.wait_ge(mem.h2T_ready, 1)
                        pe.wait_ge(mem.wq_first_in, 16)
                        experts.ask(0, 0)
                    if final and m == FIRST_FROM + 3:
                        experts.match_keys(0)
                if not final:
                    pe.wait_ge(product_done, g * N_ALL + N_ALL)
                    pe.sem_inc(split_free, 1)

            run_groups(pe, group)

        @block.scalar
        def _(act):
            chain = Chain(act, act_chain)
            experts = expert_scalar(act, mem, mem.first_work, chain)
            act.wait_ge(consts_set, 1)

            squares = lflat[:, HEADS * P:]

            def norm(g, t):
                act.wait_ge(x_loaded[t], 16 * g + 16)
                chain.step(act.activation(squares, x[:, t, :], ACT.Square, accum_out=ss[:, t:t + 1]))
                act.activation(rms[:, t:t + 1], ss[:, t:t + 1], ACT.Sqrt, bias=eps[:, 0:1],
                               scale=1.0 / D).then_inc(rms_ready, 1)

            def hT_high_part(g, t):
                for half in range(2):
                    act.wait_ge(turned_done, g * (2 * GT) + 2 * t + half + 1)
                    part = slice(half * WB, (half + 1) * WB)
                    act.activation(hT_high[:, part, t * P:(t + 1) * P], turned[:, part, :], ACT.Copy).then_inc(hT_high_ready, 1)

            def high(g, n):
                if n >= CHUNKS:
                    return
                r, s = divmod(n if n < QKV_CHUNKS else n + SLOTS - QKV_CHUNKS, SLOTS)
                act.wait_ge(stage_loaded[s % STAGES], stage_loads(g, r, s) * 16 + 16)
                act.wait_ge(split_free, g * CHUNKS + (n + 1))
                act.activation(w_high[:, n % SPLITS, :], stage[:, s % STAGES, :], ACT.Copy).then_inc(high_ready, 1)

            norm(0, 0)
            norm(0, 1)
            for t in range(GT):
                if t < GT - 2:
                    norm(0, t + 2)
                else:
                    high(0, t - (GT - 2))
                hT_high_part(0, t)

            def group(g, final):
                chain.restart()

                def product(n):
                    act.wait_ge(product_done, g * N_ALL + (n + 1))
                    return bank[:, n % BANKS, :]

                for b in range(WB):
                    act.activation(qT[:, b, :], product(N_Q + b), ACT.Copy, scale=HD ** -0.5).then_inc(act_taken, 1)
                    high(g, b + 2)
                act.wait_ge(carry_ready, g + 1)
                act.activation(kT[:, P:], product(N_K), ACT.Copy).then_inc(act_taken, 1)
                high(g, WB + 2)
                act.activation(vtok[:, 1:, :], product(N_V).rearrange("p (t m) -> p t m", t=GT),
                               ACT.Copy).then_inc(act_taken, 1)
                high(g, WB + 3)
                act.wait_ge(merged_stored, 32 * g + 32)
                for b in range(WB):
                    act.activation(guT[:, b, :], product(N_GU + b), ACT.Gelu_apprx_tanh).then_inc(act_taken, 1)
                    high(g, QKV_CHUNKS + b + 2)
                for c in range(WB, SLOTS - 1):
                    high(g, QKV_CHUNKS + c + 2)
                for t in range(GT):
                    act.activation(gv[:, t, :], product(N_GV + t), ACT.Gelu_apprx_tanh).then_inc(act_taken, 1)
                high(g, QKV_CHUNKS + SLOTS + 1)
                act.wait_ge(ln_var, g + 1)
                act.activation(ln_std[:], mv[:, :, 1], ACT.Sqrt, bias=eps[:, 0:1]).then_inc(ln_std_ready, 1)
                for t in range(GT):
                    for c in range(GATES_PER_TILE):
                        if c == 1:
                            act.wait_ge(shifted_ready, g * GT + t + 1)
                            act.activation(probs[:], probs[:], ACT.Exp).then_inc(exp_done, 1)
                        n = GATES_PER_TILE * t + c
                        act.activation(gates[:, n, :], product(N_GATE + n), ACT.Sigmoid).then_inc(act_taken, 1)
                        high(g, chunk_number(2, 0) + n + 2)
                for m in range(KO - 2):
                    high(g, chunk_number(4, 0) + m + 2)
                    if final and m == FIRST_FROM - 1:
                        experts.norm_in(0)
                    if final and m == FIRST_FROM:
                        experts.take_turned(0)
                    if final and m == FIRST_FROM + 2:
                        experts.take_query(0)
                    if final:
                        continue
                    if m == 0:
                        act.wait_ge(branch_in, g * (2 * GT) + 2 * GT)
                    if m < GT:
                        norm(g + 1, m)
                    if TURN_FROM <= m < TURN_FROM + GT:
                        hT_high_part(g + 1, m - TURN_FROM)
                if not final:
                    high(g + 1, 0)
                    high(g + 1, 1)
                else:
                    experts.take_turned_query(0)
                    experts.take_scores(0)
                    experts.numerators(0)

            run_groups(act, group)

        @block.vector
        def _(dve):
            chain = Chain(dve, dve_chain)
            step = chain.step
            experts = expert_vector(dve, mem, mem.first_work, chain)
            dve.memset(eps[:], EPS).then_inc(consts_set, 1)
            dve.sem_inc(mem.scores_free, 1)
            dve.sem_inc(dve_taken, BANKS)
            dve.wait_ge(table_done, 1)
            dve.tensor_copy(by_distance, bank[0:HEADS, BANKS - 1, 0:2 * P]).then_inc(table_out, 1)
            chain.mark(dve.memset(kT[:, 0:P], 0.0))
            chain.mark(dve.memset(before_first[:], NEG_INF))
            dve.memset(vtok[:, 0, :], 0.0).then_inc(carry_ready, 1)
            dve.wait_ge(params_in, 16)

            lnw = par[:, C_LNW:C_LNW + WIDTH]
            lnb = par[:, C_LNB:C_LNB + WIDTH]
            bs = par[:, C_BS:C_BS + WB * P].rearrange("p (b t) -> p b t", b=WB)
            sinks = par[:, C_SINK:C_SINK + HEADS]
            pm = probs[:, 0:HEADS * P].rearrange("p (h j) -> p h j", h=HEADS)
            psink = probs[:, HEADS * P:]

            def over_keys(a):
                return a.unsqueeze(2).to_broadcast([P, HEADS, P])

            def norm(g, t):
                dve.wait_ge(rms_ready, g * GT + t + 1)
                step(dve.reciprocal(rstd[:, t:t + 1], rms[:, t:t + 1]))
                dve.scalar_tensor_tensor(out=x[:, t, :], in0=x[:, t, :], scalar=rstd[:, t:t + 1], in1=par[:, C_MIXW:C_MIXW + D],
                                         op0=ALU.mult, op1=ALU.mult).then_inc(hn_ready, 1)

            def hT_low_part(g, t):
                for half in range(2):
                    part = slice(half * WB, (half + 1) * WB)
                    cols = slice(t * P, (t + 1) * P)
                    dve.wait_ge(hT_high_ready, g * (2 * GT) + 2 * t + half + 1)
                    dve.tensor_tensor(hT_low[:, part, cols], turned[:, part, :], hT_high[:, part, cols].bitcast(F32),
                                      ALU.subtract).then_inc(hT_ready, 1)

            for t in range(GT):
                norm(0, t)
                if t > 0:
                    hT_low_part(0, t - 1)
            hT_low_part(0, GT - 1)
            dve.wait_ge(late_params_in, 16)
            ws = par[:, C_WS:C_WS + HEADS * P].rearrange("p (g t) -> p g t", g=HEADS)
            own01 = par[:, C_OWN01:C_OWN01 + P].unsqueeze(1).to_broadcast([P, HEADS, P])
            prev01 = par[:, C_PREV01:C_PREV01 + P].unsqueeze(1).to_broadcast([P, HEADS, P])
            chain.mark(dve.tensor_tensor(ws, ws, own01, ALU.mult))
            dve.wait_ge(rel_done, 1)
            rel_hj = rel.rearrange("p (h j) -> p h j", h=HEADS)
            chain.mark(dve.tensor_tensor(bias_own, rel_hj, par[:, C_OWNNEG:C_OWNNEG + P].unsqueeze(1).to_broadcast([P, HEADS, P]), ALU.add))
            dve.tensor_tensor(bias_prev, rel_hj, par[:, C_PREVNEG:C_PREVNEG + P].unsqueeze(1).to_broadcast([P, HEADS, P]),
                              ALU.add).then_inc(bias_ready, 1)
            dve.wait_ge(bias_ready, 1)
            chain.wait()
            chain.restart()

            def group(g, final):
                for t in range(GT):
                    dve.wait_ge(act_taken, g * N_BRANCH + (N_GV + t + 1))
                    chain.mark(dve.bn_stats(stats[:, t, :], gv[:, t, :]))
                chain.wait()
                for t in range(GT):
                    last = dve.bn_aggr(mv[:, t, :], stats[:, t, :])
                last.then_inc(ln_var, 1)
                dve.wait_ge(ln_std_ready, g + 1)
                step(dve.reciprocal(ln_rstd[:], ln_std[:]))
                for t in range(GT):
                    dve.wait_ge(logits_done, g * GT + t + 1)
                    chain.mark(dve.tensor_tensor(pm, logits[:, :, P:2 * P], bias_own, ALU.add))
                    if t == 0:
                        step(dve.scalar_tensor_tensor(out=pt_own, in0=logits[:, :, 0:P], scalar=before_first[:, 0:1],
                                                      in1=bias_prev, op0=ALU.add, op1=ALU.add))
                    else:
                        step(dve.tensor_tensor(pt_own, logits[:, :, 0:P], bias_prev, ALU.add))
                    step(dve.tensor_tensor(pm, pm, pt_own, ALU.max))
                    step(dve.tensor_reduce(top[:], pm, AX.X, ALU.max))
                    step(dve.tensor_tensor(top[:], top[:], sinks, ALU.max))
                    chain.mark(dve.tensor_tensor(psink, sinks, top[:], ALU.subtract))
                    dve.tensor_tensor(pm, pm, over_keys(top[:]), ALU.subtract).then_inc(shifted_ready, 1)
                    step(dve.tensor_scalar(gv[:, t, :], gv[:, t, :], mv[:, t, 0:1], ln_rstd[:, t:t + 1],
                                           ALU.subtract, ALU.mult))
                    step(dve.tensor_tensor(gv[:, t, :], gv[:, t, :], lnw, ALU.mult))
                    dve.tensor_tensor(gv[:, t, :], gv[:, t, :], lnb, ALU.add).then_inc(vln_ready, 1)
                    dve.wait_ge(exp_done, g * GT + t + 1)
                    step(dve.tensor_reduce(den[:], pm, AX.X, ALU.add))
                    step(dve.tensor_tensor(den[:], den[:], psink, ALU.add))
                    step(dve.reciprocal(rden[:], den[:]))
                    dve.tensor_tensor(pm, pm, over_keys(rden[:]), ALU.mult).then_inc(probs_ready, 1)
                    dve.wait_ge(pt_done, g * GT + t + 1)
                    chain.mark(dve.tensor_tensor(pt_own, ptT, own01, ALU.mult))
                    dve.tensor_tensor(pt_prev, ptT, prev01, ALU.mult).then_inc(pt_masked, 1)
                    cols = slice(t * P, (t + 1) * P)
                    dve.wait_ge(sg_done, g * GT + t + 1)
                    gated = gv[:, t, :].rearrange("p (b i) -> p b i", b=WB)
                    step(dve.tensor_tensor(gated, sg, bs, ALU.add))
                    step(dve.tensor_tensor(gated, gated, guT[:, :, cols], ALU.mult))
                    step(dve.tensor_copy(gmlpT_high[:, :, cols], gated))
                    dve.tensor_tensor(gmlpT_low[:, :, cols], gated, gmlpT_high[:, :, cols].bitcast(F32),
                                      ALU.subtract).then_inc(branch_in, 1)
                    dve.wait_ge(pv_done, g * GT + t + 1)
                    step(dve.tensor_copy(attnT_high[:, :, cols], pv))
                    dve.tensor_tensor(attnT_low[:, :, cols], pv, attnT_high[:, :, cols].bitcast(F32),
                                      ALU.subtract).then_inc(branch_in, 1)

                if not final:
                    step(dve.tensor_copy(kT[:, 0:P], kT[:, GROUP:GROUP + P]))
                    step(dve.memset(before_first[:], 0.0))
                    dve.tensor_copy(vtok[:, 0, :], vtok[:, GT, :]).then_inc(carry_ready, 1)

                dve.wait_ge(act_taken, g * N_BRANCH + N_BRANCH)
                for m in range(KO):
                    for br in range(2):
                        n = N_BRANCH + 2 * m + br
                        dve.wait_ge(product_done, g * N_ALL + (n + 1))
                        gate = gates[:, br * KO + m, :]
                        dve.tensor_tensor(gate, gate, bank[:, n % BANKS, :], ALU.mult).then_inc(dve_taken, 1)
                    dve.wait_ge(dve_taken, g * (N_ALL - N_BRANCH) + (2 * m + 2 + BANKS))
                    dve.tensor_tensor(merged[:, :, m, :], gates[:, m, :].rearrange("p (t m) -> p t m", t=GT),
                                      gates[:, KO + m, :].rearrange("p (t m) -> p t m", t=GT), ALU.add).then_inc(merged_ready, 1)
                    if not final and m < GT:
                        norm(g + 1, m)
                    if not final and TURN_FROM <= m < TURN_FROM + GT:
                        hT_low_part(g + 1, m - TURN_FROM)
                    if final and m == FIRST_FROM:
                        experts.residual(0)
                        dve.wait_ge(mem.expert_params_in, 16)
                        experts.norm_in(0)
                    if final and m == FIRST_FROM + 3:
                        experts.best_of_sets(0)
                        experts.best_of_sums()
                if final:
                    experts.indices(0)
                    experts.normalise(0, 0)
                chain.restart()

            run_groups(dve, group)


def expert_block(nc, mem, x_in, merged_in, experts_in, w_query, out):
    with ExitStack() as ctx:
        def sb(name, shape, dt=F32):
            return ctx.enter_context(nc.sbuf_tensor(name, shape, dt))

        def sem(name):
            return ctx.enter_context(nc.semaphore(name))

        rows, xt, mt, y, par = mem.rows, mem.xt, mem.mt, mem.y, mem.par
        index, gate, turned = mem.index, mem.gate, mem.turned
        hcur = sb("hcur", [P, D])
        x3 = sb("x3", [P, D])
        work = mem.work_in(sb("work", [P, 4 * NKEYS + 2 * TOPK * TOPK]))
        dots = sb("dots", [P, 2, TOPK])
        gelu = sb("gelu", [P, 2, TOPK])
        diag = sb("diag", [P, RING, P])
        ss3 = sb("ss3", [P, 1])
        rms3 = sb("rms3", [P, 1])
        rstd3 = sb("rstd3", [P, 1])
        eps = mem.eps

        ident = par[:, E_IDENT:E_IDENT + P]

        xt_free = sem("xt_free")
        xt_claimed = sem("xt_claimed")
        row_landed = [sem(f"row_landed{s}") for s in range(RING)]
        row_free = sem("row_free")
        slot_claimed = sem("slot_claimed")
        dots_ready = sem("dots_ready")
        gelu_ready = sem("gelu_ready")
        diag_ready = sem("diag_ready")
        y_free = sem("y_free")
        rms3_ready = sem("rms3_ready")
        x3_free = sem("x3_free")
        x3_ready = sem("x3_ready")
        out_stored = sem("out_stored")
        dve_chain = sem("expert_dve_chain")
        act_chain = sem("expert_act_chain")

        block = ctx.enter_context(nc.Block())


        @block.sync
        def _(sp):
            sp.wait_ge(mem.merged_stored, 32 * (GROUPS + 1))
            sp.dma_start(mem.wq[:, 6:PH], w_query[:, 6:PH]).then_inc(mem.wq_last_in, 16)
            sp.sem_inc(x3_free, 1)
            with sp.Fori(0, TILES) as t:
                following = (t + 1) & (TILES - 1)
                sp.wait_ge(xt_free, t + 1)
                sp.sem_inc(xt_claimed, 1)
                sp.dma_start(xt, x_in[bass.ds(following, 1)].rearrange("t p d -> (t p) d")).then_inc(mem.xt_loaded, 16)
                sp.dma_start(mt.rearrange("p k m -> p (k m)"), merged_in[bass.ds(following, 1)].rearrange(
                    "t p d -> (t p) d")).then_inc(mem.mt_loaded, 16)
                sp.wait_ge(x3_ready, t + 2)
                sp.dma_start(out[bass.ds(t, 1)].rearrange("t p d -> (t p) d"), x3[:]).then_inc(out_stored, 16)
                sp.wait_ge(out_stored, 16 * t + 16)
                sp.sem_inc(x3_free, 1)
            sp.wait_ge(out_stored, 16 * TILES)

        @block.gpsimd
        def _(pool):
            with pool.Fori(0, TILES * PH // 2) as pair:
                for j in range(2):
                    i = pair * 2 + j
                    pool.wait_ge(mem.index_ready, i + 1)
                    for k in range(TOPK):
                        s = k % RING
                        pool.wait_ge(row_free, i * TOPK + (k + 1))
                        pool.sem_inc(slot_claimed, 1)
                        pool.indirect_dma_start(
                            out=rows[:, s, :], out_offset=None, in_=experts_in,
                            in_offset=bass.IndirectOffsetOnAxis(ap=index[:, j, k:k + 1], axis=0),
                        ).then_inc(row_landed[s], 16)

        @block.tensor
        def _(pe):
            ex = expert_tensor(pe, mem, work)
            pe.sem_inc(row_free, RING)

            def add_rows(i, slots):
                for k in slots:
                    s = k % RING
                    pe.wait_ge(diag_ready, i * TOPK + (k + 1))
                    for c in range(2):
                        last = pe.matmul(y[:, c, :], diag[:, s, :], rows[:, s, D + c * GROUP:D + (c + 1) * GROUP],
                                         start=False, stop=False, skip_group_check=True)
                    last.then_inc(row_free, 1)

            def score(i, h):
                ex.ask(i, h)
                ex.turn_query(i)
                ex.match_keys(i)

            early, late = range(3 * BATCH), range(3 * BATCH, TOPK)
            score(1, 1)
            pe.wait_ge(mem.wq_middle_in, 16)
            pe.wait_ge(mem.wq_late_in, 16)
            with pe.Fori(0, TILES) as t:
                pe.wait_ge(y_free, t + 1)
                for c in range(2):
                    last = pe.matmul(y[:, c, :], ident, xt[:, c * GROUP:(c + 1) * GROUP], start=True, stop=True)
                last.then_inc(xt_free, 1)
                with pe.Fori(0, PH - 2) as h:
                    add_rows(t * PH + h, early)
                    pe.wait_ge(mem.wq_last_in, 16)
                    score(t * PH + h + 2, h + 2)
                    add_rows(t * PH + h, late)
                ex.mix(t + 1, range(0, 1))
                add_rows(t * PH + (PH - 2), range(2 * BATCH))
                ex.mix(t + 1, range(1, 2))
                add_rows(t * PH + (PH - 2), range(2 * BATCH, 6 * BATCH))
                ex.turn(t + 1)
                add_rows(t * PH + (PH - 2), range(6 * BATCH, 7 * BATCH))
                pe.wait_ge(mem.h2T_ready, t + 2)
                score(t * PH + PH, 0)
                add_rows(t * PH + (PH - 2), range(7 * BATCH, TOPK))
                add_rows(t * PH + (PH - 1), early)
                score(t * PH + (PH + 1), 1)
                add_rows(t * PH + (PH - 1), late)

        @block.scalar
        def _(act):
            chain = Chain(act, act_chain)
            ex = expert_scalar(act, mem, work, chain)
            squares = turned.rearrange("p k m -> p (k m)")

            def score(i):
                ex.take_query(i)
                ex.take_turned_query(i)
                ex.take_scores(i)

            def gelus(i, j, batches):
                for b in batches:
                    cols = slice(b * BATCH, (b + 1) * BATCH)
                    act.wait_ge(dots_ready, i * BATCHES + (b + 1))
                    act.activation(gelu[:, j, cols], dots[:, j, cols], ACT.Gelu_apprx_tanh).then_inc(gelu_ready, 1)

            early, late = range(BATCHES // 2), range(BATCHES // 2, BATCHES)

            def head(i, j):
                gelus(i, j, early)
                ex.numerators(i + 1)
                score(i + 2)
                gelus(i, j, late)

            score(1)
            with act.Fori(0, TILES) as t:
                chain.restart()
                with act.Fori(0, (PH - 2) // 2) as pair:
                    for j in range(2):
                        head(t * PH + pair * 2 + j, j)
                gelus(t * PH + (PH - 2), 0, early)
                ex.norm_in(t + 1)
                ex.numerators(t * PH + (PH - 1))
                gelus(t * PH + (PH - 2), 0, late[:2])
                ex.take_turned(t + 1)
                gelus(t * PH + (PH - 2), 0, late[2:3])
                score(t * PH + PH)
                gelus(t * PH + (PH - 2), 0, late[3:])
                head(t * PH + (PH - 1), 1)
                act.wait_ge(row_free, t * (PH * TOPK) + (PH * TOPK + RING))
                act.wait_ge(x3_free, t + 1)
                act.activation(x3[:], y.rearrange("p c m -> p (c m)"), ACT.Copy).then_inc(y_free, 1)
                act.wait_ge(y_free, t + 2)
                chain.step(act.activation(squares, x3[:], ACT.Square, accum_out=ss3[:]))
                act.activation(rms3[:], ss3[:], ACT.Sqrt, bias=eps[:, 0:1], scale=1.0 / D).then_inc(rms3_ready, 1)

        @block.vector
        def _(dve):
            chain = Chain(dve, dve_chain)
            step = chain.step
            ex = expert_vector(dve, mem, work, chain)
            dve.sem_inc(y_free, 1)

            def diagonals(i, j, b):
                dve.wait_ge(gelu_ready, i * BATCHES + (b + 1))
                for k in range(b * BATCH, (b + 1) * BATCH):
                    dve.tensor_scalar(diag[:, k % RING, :], ident, gelu[:, j, k:k + 1], gate[:, j, k:k + 1],
                                      ALU.mult, ALU.mult).then_inc(diag_ready, 1)

            def finish(t):
                dve.wait_ge(rms3_ready, t + 2)
                step(dve.reciprocal(rstd3[:], rms3[:]))
                step(dve.scalar_tensor_tensor(out=x3[:], in0=x3[:], scalar=rstd3[:, 0:1], in1=par[:, E_FINW:E_FINW + D],
                                              op0=ALU.mult, op1=ALU.mult))
                dve.sem_inc(x3_ready, 1)

            def head(i, j, following=None, finished=None):
                for b in range(BATCHES):
                    for k in range(b * BATCH, (b + 1) * BATCH):
                        dve.wait_ge(row_landed[k % RING], 16 * (TOPK // RING) * i + 16 * (k // RING + 1))
                        u = rows[:, k % RING, 0:D]
                        last = dve.tensor_tensor_reduce(out=u, in0=u, in1=hcur[:], scale=1.0,
                                                        scalar=0.0, op0=ALU.mult, op1=ALU.add, accum_out=dots[:, j, k:k + 1])
                    last.then_inc(dots_ready, 1)
                    if b > 0:
                        diagonals(i, j, b - 1)
                    if finished is not None and b == FINISH_AT:
                        finish(finished)
                    if b == 1:
                        ex.best_of_sets(i + 1)
                    if b == 2:
                        ex.best_of_sums()
                    if b == 3:
                        ex.indices(1 - j)
                    if following is not None and b == 3:
                        ex.residual(following)
                    if following is not None and b == 5:
                        ex.norm_in(following)
                    if b == BATCHES - 2:
                        ex.normalise(i + 1, 1 - j)
                diagonals(i, j, BATCHES - 1)

            step(dve.tensor_copy(hcur[:], mem.hnext))
            chain.mark(dve.memset(x3[:], 0.0))
            step(dve.memset(rms3[:], 1.0))
            dve.sem_inc(rms3_ready, 1)
            with dve.Fori(0, TILES) as t:
                chain.restart()
                head(t * PH, 0, finished=t - 1)
                head(t * PH + 1, 1)
                with dve.Fori(1, (PH - 2) // 2) as pair:
                    chain.restart()
                    for j in range(2):
                        head(t * PH + pair * 2 + j, j)
                chain.restart()
                head(t * PH + (PH - 2), 0, following=t + 1)
                head(t * PH + (PH - 1), 1)
                step(dve.tensor_copy(hcur[:], mem.hnext))
            finish(TILES - 1)



def distance_buckets():
    n = np.arange(P)
    exact = BUCKETS // 2
    large = exact + (np.log(np.maximum(n, 1) / exact) / np.log(MAX_DISTANCE / exact) * (BUCKETS - exact)).astype(np.int32)
    return np.where(n < exact, n, np.minimum(large, BUCKETS - 1))


def mixer_params(a):
    par = np.zeros((P, MIX_COLS), np.float32)
    i = np.arange(P)
    par[:, C_MIXW:C_SINK] = a["mix_norm_w"][0]
    par[:, C_SINK:C_LNW] = a["attn_sinks"][0]
    par[:, C_LNW:C_LNB] = a["gmlp_ln_w"][0]
    par[:, C_LNB:C_BS] = a["gmlp_ln_b"][0]
    par[:, C_BS:C_WS] = np.repeat(a["gmlp_b_s"][0].reshape(WB, 2, P).transpose(1, 0, 2).reshape(2, WB * P), HD, axis=0)
    par[:, C_WS:C_OWN01] = a["gmlp_w_s"][0].transpose(2, 0, 1).reshape(P, HEADS * P)
    par[:, C_IDENT:C_MIXW] = np.eye(P)
    par[:, C_OWN01:C_PREV01] = i[:, None] <= i[None, :]
    par[:, C_PREV01:C_OWNNEG] = i[:, None] > i[None, :]
    par[:, C_OWNNEG:C_PREVNEG] = np.where(i[None, :] > i[:, None], NEG_INF, 0)
    par[:, C_PREVNEG:] = np.where(i[None, :] <= i[:, None], NEG_INF, 0)
    return par


def rel_params(a):
    par = np.zeros((P, REL_COLS), np.float32)
    distance = (P - 1 - np.arange(2 * P)) % P
    par[:BUCKETS, R_DIST:R_REL] = distance_buckets()[distance][None] == np.arange(BUCKETS)[:, None]
    par[:BUCKETS, R_REL:R_FLIP] = a["rel_bias"]
    par[:, R_FLIP:] = np.eye(P)[::-1]
    return par


def mixer_weights(a):
    w_in = a["w_in"][0]
    q0, k0, v0, gu0, gv0, g0 = np.cumsum([0, WIDTH, KV_HEADS * HD, KV_HEADS * HD, WIDTH, WIDTH])
    chunks = np.zeros((ROUNDS * SLOTS, P, CHUNK), np.float32)

    def blocks(w):
        return w.reshape(KO, P, -1, P).transpose(2, 1, 0, 3).reshape(-1, P, CHUNK)

    def pairs(w):
        return w.reshape(KO // 2, 2, P, GROUP).transpose(0, 2, 1, 3).reshape(-1, P, CHUNK)

    wq = w_in[:, q0:k0].reshape(D, 2, WB, HD).transpose(0, 2, 1, 3).reshape(D, WIDTH)
    chunks[0:WB] = blocks(wq)
    chunks[WB:WB + 1] = blocks(w_in[:, k0:v0])
    chunks[WB + 1:WB + 2] = blocks(w_in[:, v0:gu0])
    chunks[SLOTS:SLOTS + WB] = blocks(w_in[:, gu0:gv0])
    chunks[SLOTS + WB:2 * SLOTS] = pairs(w_in[:, gv0:g0])
    chunks[2 * SLOTS:4 * SLOTS] = blocks(w_in[:, g0:])
    wa = a["w_branch_attn"][0].reshape(2, WB, HD, D).transpose(1, 0, 2, 3).reshape(WIDTH, D)
    both = np.stack([wa, a["w_branch_gmlp"][0]]).reshape(2, WB, P, KO, P)
    chunks[4 * SLOTS:5 * SLOTS] = both.transpose(3, 2, 0, 1, 4).reshape(KO, P, CHUNK)
    return chunks


def expert_params(a):
    par = np.zeros((P, EXP_COLS), np.float32)
    par[:, E_KEYS:E_KEYS + NKEYS] = a["peer_keys_1"][0].T
    par[:, E_KEYS + NKEYS:E_IDENT] = a["peer_keys_2"][0].T
    par[:, E_IDENT:E_FFNW] = np.eye(P)
    par[:, E_FFNW:E_FINW] = a["ffn_norm_w"][0]
    par[:, E_FINW:E_IOTA] = a["final_norm_w"]
    par[:, E_IOTA:] = np.arange(TOPK)
    return par


def kernel(**inputs):
    import concourse.bacc as _bacc
    from concourse.bass_utils import run_bass_kernel_spmd as _run

    a = {k: np.asarray(v) for k, v in inputs.items()}
    arrays = {
        "x": a["x"][0].reshape(TILES, P, D),
        "weights": mixer_weights(a),
        "mix_params": mixer_params(a),
        "rel_params": rel_params(a),
        "experts": np.ascontiguousarray(np.concatenate([a["peer_u"][0], a["peer_v"][0]], axis=1)),
        "w_out": np.ascontiguousarray(a["w_out"][0].reshape(KO, P, D).transpose(1, 0, 2)),
        "w_query": np.ascontiguousarray(a["peer_w_q"][0].reshape(KO, P, PH, 2 * NKEYS).transpose(1, 2, 0, 3)),
        "exp_params": expert_params(a),
    }
    nc = _bacc.Bacc("TRN2", target_bir_lowering=False, num_devices=1)
    d = {n: nc.dram_tensor(f"in_{n}", v.shape, F32, kind="ExternalInput").ap() for n, v in arrays.items()}
    merged = nc.dram_tensor("merged_branches", (TILES, P, D), F32, kind="Internal").ap()
    rel_table = nc.dram_tensor("rel_table", (HEADS, 2 * P), F32, kind="Internal").ap()
    out = nc.dram_tensor("out", (1, SEQ, D), F32, kind="ExternalOutput").ap()
    with ExitStack() as ctx:
        mem = shared_memory(nc, ctx)
        mixer_block(nc, mem, d["x"], d["weights"], d["mix_params"], d["rel_params"], rel_table,
                    d["w_out"], d["w_query"], d["exp_params"], merged)
        expert_block(nc, mem, d["x"], merged, d["experts"], d["w_query"],
                     out[0].rearrange("(t p) d -> t p d", p=P))
    r = _run(nc, [{f"in_{n}": v for n, v in arrays.items()}], core_ids=[0])
    return r.results[0]["out"]
```
